# Optimizing a Trainium2 kernel written in Bass

```python
import jax, jax.numpy as jnp
from jax import lax
import numpy as np

D_MODEL = 1024
BATCH = 1
SEQ = 512
DEPTH = 2

N_MIXERS = 2
N_A_LAYERS = (DEPTH + 1) // 2
N_B_LAYERS = DEPTH // 2
CONV_KERNEL = 31
POOL_WINDOWS = (2, 4, 8, 16)
N_POOL_GROUPS = len(POOL_WINDOWS)
POOL_GROUP_DIM = D_MODEL // N_POOL_GROUPS
D_FF = ((8 * D_MODEL // 3 + 127) // 128) * 128
FFN_CONV_KERNEL = 3
RMS_EPS = 1e-6
LN_EPS = 1e-5

kernel_name = "hybrid_conformerconv_msnpool_convffn"

def rmsnorm(x, g):
    xf = x.astype(jnp.float32)
    y = xf * lax.rsqrt(jnp.mean(xf * xf, axis=-1, keepdims=True) + RMS_EPS)
    return (y * g.astype(jnp.float32)).astype(x.dtype)

def layernorm(x, g, b):
    xf = x.astype(jnp.float32)
    mu = jnp.mean(xf, axis=-1, keepdims=True)
    var = jnp.mean(jnp.square(xf - mu), axis=-1, keepdims=True)
    y = (xf - mu) * lax.rsqrt(var + LN_EPS)
    return (y * g.astype(jnp.float32) + b.astype(jnp.float32)).astype(x.dtype)

def causal_dwconv(x, w, b):
    k, c = w.shape
    y = lax.conv_general_dilated(
        x, w[:, None, :].astype(x.dtype),
        window_strides=(1,), padding=((k - 1, 0),),
        dimension_numbers=("NWC", "WIO", "NWC"),
        feature_group_count=c)
    return y + b

def conformer_conv_module(h, w_pw1, b_pw1, w_dw, b_dw, ln_g, ln_b, w_pw2, b_pw2):
    d = h.shape[-1]
    a = jnp.einsum("bsd,de->bse", h, w_pw1) + b_pw1
    u = a[..., :d] * jax.nn.sigmoid(a[..., d:])
    u = causal_dwconv(u, w_dw, b_dw)
    u = jax.nn.silu(layernorm(u, ln_g, ln_b))
    return jnp.einsum("bsd,de->bse", u, w_pw2) + b_pw2

def multiscale_pool_mixer(h, w_grp, b_grp, scale):
    bsz, s, d = h.shape
    hf = h.astype(jnp.float32)
    cs = jnp.concatenate(
        [jnp.zeros((bsz, 1, d), jnp.float32), lax.cumsum(hf, axis=1)], axis=1)
    t = jnp.arange(s)
    outs = []
    for g, w in enumerate(POOL_WINDOWS):
        sl = slice(g * POOL_GROUP_DIM, (g + 1) * POOL_GROUP_DIM)
        c = cs[..., sl]
        lagged = jnp.pad(c[:, : s + 1 - w], ((0, 0), (w - 1, 0), (0, 0)))
        win_sum = c[:, 1:] - lagged
        cnt = jnp.minimum(t + 1, w).astype(jnp.float32)[None, :, None]
        outs.append(win_sum / cnt - hf[..., sl])
    pooled = jnp.stack(outs, axis=2).astype(h.dtype)
    mixed = jnp.einsum("bsgc,gce->bsge", pooled, w_grp).reshape(bsz, s, d)
    return scale * (mixed + b_grp)

def conv_ffn(h, w_up, w_dw, b_dw, w_down):
    up = jnp.einsum("bsd,df->bsf", h, w_up)
    act, gate = up[..., :D_FF], up[..., D_FF:]
    act = causal_dwconv(act, w_dw, b_dw)
    return jnp.einsum("bsf,fd->bsd", jax.nn.silu(act) * gate, w_down)

def setup_inputs(seed: int = 0) -> dict:
    key = jax.random.key(seed)
    ks = jax.random.split(key, 24)
    f32 = jnp.float32
    D, G, Cg = D_MODEL, N_POOL_GROUPS, POOL_GROUP_DIM
    nrm = lambda k, shape, sc: jax.random.normal(k, shape, f32) * sc
    gain = lambda k, shape: 1.0 + 0.05 * jax.random.normal(k, shape, f32)
    return {
        "x": jax.random.normal(ks[0], (BATCH, SEQ, D), f32),
        "norm_mix": gain(ks[1], (DEPTH, D)),
        "norm_ffn": gain(ks[2], (DEPTH, D)),
        "conv_w_pw1": nrm(ks[3], (N_A_LAYERS, D, 2 * D), D ** -0.5),
        "conv_b_pw1": nrm(ks[4], (N_A_LAYERS, 2 * D), 0.02),
        "conv_w_dw": nrm(ks[5], (N_A_LAYERS, CONV_KERNEL, D), CONV_KERNEL ** -0.5),
        "conv_b_dw": nrm(ks[6], (N_A_LAYERS, D), 0.02),
        "conv_ln_g": gain(ks[7], (N_A_LAYERS, D)),
        "conv_ln_b": nrm(ks[8], (N_A_LAYERS, D), 0.02),
        "conv_w_pw2": nrm(ks[9], (N_A_LAYERS, D, D), D ** -0.5),
        "conv_b_pw2": nrm(ks[10], (N_A_LAYERS, D), 0.02),
        "pool_w": nrm(ks[11], (N_B_LAYERS, G, Cg, Cg), Cg ** -0.5),
        "pool_b": nrm(ks[12], (N_B_LAYERS, D), 0.02),
        "pool_scale": gain(ks[13], (N_B_LAYERS, D)),
        "ffn_w_up": nrm(ks[14], (DEPTH, D, 2 * D_FF), D ** -0.5),
        "ffn_w_dw": nrm(ks[15], (DEPTH, FFN_CONV_KERNEL, D_FF), FFN_CONV_KERNEL ** -0.5),
        "ffn_b_dw": nrm(ks[16], (DEPTH, D_FF), 0.02),
        "ffn_w_down": nrm(ks[17], (DEPTH, D_FF, D), D_FF ** -0.5),
        "final_norm": gain(ks[18], (D,)),
    }

def reference(x, norm_mix, norm_ffn, conv_w_pw1, conv_b_pw1, conv_w_dw, conv_b_dw,
              conv_ln_g, conv_ln_b, conv_w_pw2, conv_b_pw2, pool_w, pool_b, pool_scale,
              ffn_w_up, ffn_w_dw, ffn_b_dw, ffn_w_down, final_norm):
    ia, ib = 0, 0
    for i in range(DEPTH):
        h = rmsnorm(x, norm_mix[i])
        if i % N_MIXERS == 0:
            x = x + conformer_conv_module(
                h, conv_w_pw1[ia], conv_b_pw1[ia], conv_w_dw[ia], conv_b_dw[ia],
                conv_ln_g[ia], conv_ln_b[ia], conv_w_pw2[ia], conv_b_pw2[ia])
            ia += 1
        else:
            x = x + multiscale_pool_mixer(h, pool_w[ib], pool_b[ib], pool_scale[ib])
            ib += 1
        h = rmsnorm(x, norm_ffn[i])
        x = x + conv_ffn(h, ffn_w_up[i], ffn_w_dw[i], ffn_b_dw[i], ffn_w_down[i])
    return rmsnorm(x, final_norm)


_drawn_inputs = setup_inputs


def setup_inputs(seed=0):
    import zlib

    import numpy as np

    out = dict(_drawn_inputs(seed))
    spreads = {}
    factors = {'conv_b_pw1': 4.253,
     'conv_ln_b': 5.035,
     'conv_b_pw2': 3.193,
     'pool_b': 4.289,
     'ffn_b_dw': 4.644}
    for name, (base, spread) in spreads.items():
        noise = np.random.default_rng([zlib.crc32(name.encode()), seed]).standard_normal(out[name].shape)
        drawn = base * np.exp(spread * noise) if base else spread * noise
        out[name] = __import__('jax').numpy.asarray(drawn.astype(out[name].dtype))
    for name, factor in factors.items():
        out[name] = (out[name] * factor).astype(out[name].dtype)
    return out
```

```python
import concourse.bass as bass
from concourse import mybir
from contextlib import ExitStack

P = 128
D = 1024
T = 512
FF = 2816
KD = D // P
KF = FF // P
UNIT = 8 * 2 * P
DOWN_K = KF // 2
DOWN_UNIT = DOWN_K * P
POOL_UNIT = 2 * 2 * 2 * P
TAPS = 31
PAD = TAPS - 1
WINDOWS = (2, 4, 8, 16)
RMS_EPS = 1e-6
LN_EPS = 1e-5
DEPTH = 2

PW1_STEPS = 4
PW2_STEPS = 2
UP_STEPS = KF // 2
DOWN_STEPS = KD
M_PW1 = 0
M_PW2 = M_PW1 + PW1_STEPS
M_UP = [M_PW2 + PW2_STEPS, 0]
M_DOWN = [M_UP[0] + UP_STEPS, 0]
M_POOL = M_DOWN[0] + DOWN_STEPS
M_UP[1] = M_POOL + 1
M_DOWN[1] = M_UP[1] + UP_STEPS
DRAINED_PW1, DRAINED_UP, DRAINED_POOL = 0, (PW1_STEPS, PW1_STEPS + UP_STEPS + 2), PW1_STEPS + UP_STEPS
X_PW2, X_DOWN, X_POOL = 0, (KD, 3 * KD), 2 * KD
H_IN, H_PW2, H_POOL = 0, KD, 2 * KD
Q_IN, Q_PW2, Q_DOWN, Q_POOL = 0, KD, (2 * KD, 4 * KD), 3 * KD
S_IN, S_PW2, S_DOWN, S_POOL = 0, KD + 1, (2 * (KD + 1), 4 * (KD + 1)), 3 * (KD + 1)

COL = {}
_at = 0
for _name, _n in [("mix0", KD), ("mix1", KD), ("ffn0", KD), ("ffn1", KD), ("final", KD), ("b_pw1", 2 * KD),
                  ("b_dw", KD), ("ln_g", KD), ("ln_b", KD), ("b_pw2", KD), ("pool_b", KD), ("pool_s", KD),
                  ("w_dw", KD * TAPS), ("ffn_dw", DEPTH * KF * 4)]:
    COL[_name] = _at
    _at += _n
N_COLS = _at

PE_TAPS = [12, 12, 12, 12]
DIAG_TAPS = [max(PE_TAPS[0::2]), max(PE_TAPS[1::2])]

EARLY_TAPS = 22

BANK_SUM, BANK_MEAN = 4, 7
BANKS_CONV = [(5, 6), (5, 6), (5, 6), (0, 1)]


def build(nc, x_in, vecs, ident_in, w_pw1, w_pw2, w_up, w_down, w_pool, out):
    f32, f32r = mybir.dt.float32, mybir.dt.float32r
    ALU, ACT = mybir.AluOpType, mybir.ActivationFunctionType
    MUL, ADD, SUB = ALU.mult, ALU.add, ALU.subtract

    ctx = ExitStack()
    with ctx:
        at = [nc.sbuf_base]

        def place(name, shape, dt, offset=None):
            size = 4
            for n in shape[1:]:
                size *= n
            size = (size + 31) // 32 * 32
            if offset is None:
                offset = at[0]
                at[0] += size
            return nc.alloc_sbuf_tensor_at(name, shape, dt, offset=offset)

        at[0] = (at[0] + 31) // 32 * 32
        par = place("par", [P, N_COLS], f32)
        ident = place("ident", [P, P], f32)
        ones = place("ones", [P, P], f32)
        eps = place("eps", [P, 2], f32)
        inv_count = place("inv_count", [P, 16], f32)
        x_res = place("x_res", [P, KD, T], f32)
        h_hi = place("h_hi", [P, KD, T], f32r)
        h_lo = place("h_lo", [P, KD, T], f32r)
        w_raw = [place(f"w_raw{s}", [P, UNIT], f32) for s in range(2)]
        w_hi = [place(f"w_hi{s}", [P, UNIT], f32r) for s in range(2)]
        w_lo = [place(f"w_lo{s}", [P, UNIT], f32r) for s in range(2)]
        rms = place("rms", [P, T], f32)
        sumsq = place("sumsq", [P, T], f32)
        sq = place("sq", [P, 2, T], f32)
        act_in = place("act_in", [P, 2, 2 + T], f32)
        y = place("y", [P, 2, T], f32)
        U_HI = at[0]
        u_hi = place("u_hi", [P, KF, T], f32r)
        U_LO = at[0]
        u_lo = place("u_lo", [P, KF, T], f32r)
        v_hi, v_lo = u_lo[:, 0:KD, :], u_lo[:, KD:2 * KD, :]
        conv_out = place("conv_out", [P, KD, T], f32, U_HI)
        o = U_HI + KD * T * 4
        glu = place("glu", [P, 2, PAD + T], f32, o)
        glu_hi = place("glu_hi", [P, 4, PAD + T], f32r, o + 4352)
        glu_lo = place("glu_lo", [P, 4, PAD + T], f32r, o + 4352 + 8704)
        val, gate = y, act_in[:, :, 2:2 + T]
        o_taps = o + 5 * 4352
        tap_hi = place("tap_hi", [P, KD * TAPS], f32r, o_taps)
        tap_lo = place("tap_lo", [P, KD * TAPS], f32r, o_taps + 1024)
        o_diag = [o_taps + 2048, o_taps + 2048 + 4 * DIAG_TAPS[0] * P * 4]
        diag_hi = [[place(f"diag_hi{q}{t}", [P, DIAG_TAPS[q], P], f32r, o_diag[q] + t * DIAG_TAPS[q] * P * 4)
                    for t in range(2)] for q in range(2)]
        diag_lo = [[place(f"diag_lo{q}{t}", [P, DIAG_TAPS[q], P], f32r, o_diag[q] + (2 + t) * DIAG_TAPS[q] * P * 4)
                    for t in range(2)] for q in range(2)]
        assert o_diag[1] + 4 * DIAG_TAPS[1] * P * 4 <= U_HI + 2 * KF * T * 4
        mean = place("mean", [P, T], f32, o)
        rstd = place("rstd", [P, T], f32, o + 2048)
        pool_h = place("pool_h", [P, 2, 16 + T], f32, U_HI)
        win_a = place("win_a", [P, 2, 16 + T], f32, U_HI + 4224)
        win_b = place("win_b", [P, 2, 16 + T], f32, U_HI + 2 * 4224)
        pooled = place("pooled", [P, 2, T], f32, U_HI + 3 * 4224)
        out_sb = place("out_sb", [P, KD, T], f32, U_HI)

        bank = [ctx.enter_context(nc.psum_tensor(f"bank{b}", [P, T], f32)) for b in range(8)]

        def sem(name):
            return ctx.enter_context(nc.semaphore(name))

        def sems(name, n=2):
            return [sem(f"{name}{i}") for i in range(n)]

        par_loaded, ident_loaded, out_stored = sem("par_loaded"), sem("ident_loaded"), sem("out_stored")
        x_loaded = sems("x_loaded", 4)
        raw_loaded = sems("raw_loaded")
        w_rounded = sems("w_rounded")
        w_split = sems("w_split")
        unit_done = sems("unit_done")
        drained = sems("drained", 4)
        x_updated, h_rounded, h_split = sem("x_updated"), sem("h_rounded"), sem("h_split")
        squared, summed = sem("squared"), sem("summed")
        stat_mm, root_done, rms_ready = sem("stat_mm"), sem("root_done"), sem("rms_ready")
        consts_set, memory_cleared = sem("consts_set"), sem("memory_cleared")
        taps_split, tap_rounded = sem("taps_split"), sem("tap_rounded")
        diag_ready = sems("diag_ready")
        gate_ready, glu_done = sems("gate_ready"), sems("glu_done")
        glu_rounded, glu_split = sems("glu_rounded"), sems("glu_split")
        tap_step = sems("tap_step")
        conv_mm, conv_drained = sems("conv_mm"), sem("conv_drained")
        mean_mm, mean_ready, centred = sem("mean_mm"), sem("mean_ready"), sem("centred")
        dev_squared, dev_summed = sem("dev_squared"), sem("dev_summed")
        std_ready, rstd_ready = sem("std_ready"), sem("rstd_ready")
        normed, swished, v_rounded, v_split = sem("normed"), sem("swished"), sem("v_rounded"), sem("v_split")
        tap2_done, tap1_done, conv3_done = sems("tap2_done"), sems("tap1_done"), sems("conv3_done")
        silu_done, act_scaled = sems("silu_done"), sems("act_scaled")
        u_rounded, u_split = sems("u_rounded"), sems("u_split")
        pool_step, pooled_done = sem("pool_step"), sem("pooled_done")
        out_ready = sem("out_ready")

        def col(name, i, n=1):
            return par[:, bass.ds(COL[name] + i, n)]

        def flat(ap):
            return ap.rearrange("p a t -> p (a t)")

        def chunk(tensor, c):
            return flat(tensor[:, bass.ds(c, 1), :])

        def as_f32(ap):
            return ap.bitcast(f32)

        block = ctx.enter_context(nc.Block())

        @block.sync
        def _(sp):
            sp.dma_start(par[:, :], vecs).then_inc(par_loaded, 16)
            sp.dma_start(x_res[:, 0:2, :], x_in[:, 0:2, :]).then_inc(x_loaded[0], 16)

            def load_step(source, first, m, columns, wait=True):
                for s in range(2):
                    if wait:
                        sp.wait_ge(w_split[s], m)
                    sp.dma_start(w_raw[s][:, 0:columns], source[first + s]).then_inc(raw_loaded[s], 16)

            load_step(w_pw1, 0, M_PW1, UNIT, wait=False)
            for q in range(1, 4):
                sp.dma_start(x_res[:, 2 * q:2 * q + 2, :], x_in[:, 2 * q:2 * q + 2, :]).then_inc(x_loaded[q], 16)
            sp.dma_start(ident[:, :], ident_in).then_inc(ident_loaded, 16)
            with sp.Fori(1, PW1_STEPS) as i:
                load_step(w_pw1, 2 * i, M_PW1 + i, UNIT)
            with sp.Fori(0, PW2_STEPS) as i:
                load_step(w_pw2, 2 * i, M_PW2 + i, UNIT)
            for layer in range(DEPTH):
                if layer == 1:
                    load_step(w_pool, 0, M_POOL, POOL_UNIT)
                with sp.Fori(0, UP_STEPS) as i:
                    load_step(w_up, 2 * i + 2 * UP_STEPS * layer, M_UP[layer] + i, UNIT)
                with sp.Fori(0, DOWN_STEPS) as e:
                    load_step(w_down, 2 * e + 2 * DOWN_STEPS * layer, M_DOWN[layer] + e, DOWN_UNIT)
            for c in range(KD):
                sp.wait_ge(out_ready, c + 1)
                sp.dma_start(out[:, c, :], out_sb[:, c, :]).then_inc(out_stored, 16)
            sp.wait_ge(out_stored, 16 * KD)

        @block.gpsimd
        def _(pool):
            nc.gpsimd.memset(ones[:, :], 1.0).then_inc(consts_set, 1)
            nc.gpsimd.memset(eps[:, 0:1], RMS_EPS).then_inc(consts_set, 1)
            nc.gpsimd.memset(eps[:, 1:2], LN_EPS).then_inc(consts_set, 1)
            nc.gpsimd.memset(act_in[:, :, 0:2], 0.0).then_inc(consts_set, 1)
            nc.gpsimd.memset(glu[:, :, 0:PAD], 0.0).then_inc(consts_set, 1)
            for t in range(max(WINDOWS) - 1):
                nc.gpsimd.memset(inv_count[:, t:t + 1], 1.0 / (t + 1)).then_inc(consts_set, 1)

        CONSTS = 5 + max(WINDOWS) - 1

        @block.scalar
        def _(act):
            def round_unit(s, m, columns, first=False):
                act.wait_ge(raw_loaded[s], 16 * (m + 1))
                if not first:
                    act.wait_ge(unit_done[s], m)
                nc.scalar.activation(w_hi[s][:, 0:columns], w_raw[s][:, 0:columns], ACT.Copy).then_inc(w_rounded[s], 1)

            def round_x(c, norm, s_index, t):
                if norm is not None:
                    nc.scalar.activation(chunk(h_hi, c), chunk(x_res, c), ACT.Copy, scale=col(norm, c)).then_inc(h_rounded, 1)
                act.wait_ge(summed, s_index)
                nc.scalar.activation(sq[:, t, :], chunk(x_res, c), ACT.Square).then_inc(squared, 1)

            def root(n):
                act.wait_ge(stat_mm, n + 1)
                nc.scalar.activation(rms[:, :], bank[BANK_SUM][:, :], ACT.Sqrt, scale=1.0 / D, bias=eps[:, 0:1]).then_inc(root_done, 1)

            act.wait_ge(par_loaded, 16)
            act.wait_ge(consts_set, CONSTS)
            for c in range(KD):
                act.wait_ge(x_loaded[c // 2], 16)
                round_x(c, "mix0", S_IN + max(c, 1), c % 2)
                if c == 1:
                    for s in range(2):
                        round_unit(s, M_PW1, UNIT, first=True)
                if c == 5:
                    nc.scalar.activation(tap_hi[:, :], par[:, COL["w_dw"]:COL["w_dw"] + KD * TAPS], ACT.Copy).then_inc(tap_rounded, 1)
            root(0)

            def diagonals(i, t):
                if i == 0 and t == 0:
                    act.wait_ge(ident_loaded, 16)
                    act.wait_ge(taps_split, 1)
                if i >= 2:
                    act.wait_ge(conv_mm[t], i - 1)
                for k in range(PE_TAPS[i]):
                    w = (2 * i + t) * TAPS + k
                    nc.scalar.activation(diag_hi[i % 2][t][:, k, :], ident[:, :], ACT.Copy, scale=as_f32(tap_hi[:, w:w + 1])).then_inc(diag_ready[t], 1)
                    nc.scalar.activation(diag_lo[i % 2][t][:, k, :], ident[:, :], ACT.Copy, scale=as_f32(tap_lo[:, w:w + 1])).then_inc(diag_ready[t], 1)

            for i in range(PW1_STEPS):
                if i == 0:
                    round_unit(0, M_PW1 + 1, UNIT)
                for t in range(2):
                    act.wait_ge(drained[2 + t], DRAINED_PW1 + i + 1)
                    nc.scalar.activation(gate[:, t, :], gate[:, t, :], ACT.Sigmoid, bias=col("b_pw1", KD + 2 * i + t)).then_inc(gate_ready[t], 1)
                if i:
                    round_unit(0, M_PW1 + i + 1, UNIT)
                round_unit(1, M_PW1 + i + 1, UNIT)
                for t in range(2):
                    act.wait_ge(glu_done[t], i + 1)
                    if i >= 2:
                        act.wait_ge(conv_mm[t], i - 1)
                    nc.scalar.activation(glu_hi[:, 2 * (i % 2) + t, :], glu[:, t, :], ACT.Copy).then_inc(glu_rounded[t], 1)
                for pair in ((0, 1) if i == 0 else (i + 1,) if i < PW1_STEPS - 1 else ()):
                    for t in range(2):
                        diagonals(pair, t)

            act.wait_ge(mean_mm, 1)
            nc.scalar.activation(mean[:, :], bank[BANK_MEAN][:, :], ACT.Copy, scale=1.0 / D).then_inc(mean_ready, 1)
            for c in range(KD):
                act.wait_ge(centred, c + 1)
                if c >= 2:
                    act.wait_ge(dev_summed, c - 1)
                nc.scalar.activation(sq[:, c % 2, :], conv_out[:, c, :], ACT.Square).then_inc(dev_squared, 1)
            act.wait_ge(dev_summed, KD)
            nc.scalar.activation(rstd[:, :], bank[BANK_SUM][:, :], ACT.Sqrt, scale=1.0 / D, bias=eps[:, 1:2]).then_inc(std_ready, 1)
            for c in range(KD):
                act.wait_ge(normed, c + 1)
                nc.scalar.activation(conv_out[:, c, :], conv_out[:, c, :], ACT.Silu, scale=col("ln_g", c), bias=col("ln_b", c)).then_inc(swished, 1)
                act.wait_ge(swished, c + 1)
                nc.scalar.activation(v_hi[:, c, :], conv_out[:, c, :], ACT.Copy).then_inc(v_rounded, 1)

            def pw2_step(j, next_m):
                for s in range(2):
                    for t in range(2):
                        c = 4 * j + 2 * s + t
                        act.wait_ge(x_updated, X_PW2 + c + 1)
                        round_x(c, "ffn0", S_PW2 + c, t)
                    round_unit(s, next_m, UNIT)

            for j in range(PW2_STEPS):
                pw2_step(j, M_PW2 + j + 1)

            def up_step(layer, i, columns):
                m, f = M_UP[layer], DRAINED_UP[layer]
                n = layer * UP_STEPS
                for t in range(2):
                    act.wait_ge(drained[t], f + i + 1)
                    w = COL["ffn_dw"] + 4 * (layer * KF + t) + 8 * i
                    nc.scalar.activation(y[:, t, :], act_in[:, t, 2:2 + T], ACT.Identity,
                                         scale=par[:, bass.ds(w + 2, 1)], bias=par[:, bass.ds(w + 3, 1)]).then_inc(tap2_done[t], 1)
                round_unit(0, m + i + 1, columns)
                for t in range(2):
                    act.wait_ge(conv3_done[t], n + i + 1)
                    nc.scalar.activation(y[:, t, :], y[:, t, :], ACT.Silu).then_inc(silu_done[t], 1)
                for t in range(2):
                    act.wait_ge(drained[2 + t], f + i + 1)
                    nc.scalar.activation(chunk(u_hi, 2 * i + t), y[:, t, :], ACT.Copy).then_inc(u_rounded[t], 1)
                round_unit(1, m + i + 1, columns)

            def down_step(layer, j, columns):
                m = M_DOWN[layer]
                for t in range(2):
                    round_unit(0, m + 2 * j + t + 1, columns[t])
                    act.wait_ge(x_updated, X_DOWN[layer] + 2 * j + t + 1)
                    round_x(2 * j + t, None, S_DOWN[layer] + 2 * j + t, t)
                    round_unit(1, m + 2 * j + t + 1, columns[t])

            for layer in range(DEPTH):
                if layer == 1:
                    root(2)
                    for c in range(KD):
                        act.wait_ge(pooled_done, c + 1)
                        nc.scalar.activation(v_hi[:, c, :], pooled[:, c % 2, :], ACT.Copy).then_inc(v_rounded, 1)
                    for s in range(2):
                        for e in range(4 * s, 4 * s + 4):
                            act.wait_ge(x_updated, X_POOL + e + 1)
                            round_x(e, "ffn1", S_POOL + e, e % 2)
                        round_unit(s, M_UP[1], UNIT)
                root(1 if layer == 0 else 3)
                with act.Fori(0, UP_STEPS - 1) as i:
                    up_step(layer, i, UNIT)
                up_step(layer, UP_STEPS - 1, DOWN_UNIT)
                with act.Fori(0, DOWN_STEPS // 2 - 1) as j:
                    down_step(layer, j, (DOWN_UNIT, DOWN_UNIT))
                j = DOWN_STEPS // 2 - 1
                if layer == 0:
                    down_step(layer, j, (DOWN_UNIT, POOL_UNIT))
                else:
                    m = M_DOWN[1] + 2 * j + 1
                    for t in range(2):
                        if t == 0:
                            round_unit(0, m, DOWN_UNIT)
                        act.wait_ge(x_updated, X_DOWN[1] + 2 * j + t + 1)
                        round_x(2 * j + t, None, S_DOWN[1] + 2 * j + t, t)
                        if t == 0:
                            round_unit(1, m, DOWN_UNIT)
            root(4)

        @block.vector
        def _(dve):
            V = nc.vector

            def split_unit(s, m, columns):
                dve.wait_ge(w_rounded[s], m + 1)
                V.tensor_tensor(w_lo[s][:, 0:columns], w_raw[s][:, 0:columns], as_f32(w_hi[s][:, 0:columns]), SUB).then_inc(w_split[s], 1)

            def clear_sums():
                V.memset(sumsq[:, :], 0.0).then_inc(summed, 1)

            def split_x(c, norm, h_index, q_index, s_index, t):
                if norm is not None:
                    dve.wait_ge(h_rounded, h_index + 1)
                    V.scalar_tensor_tensor(chunk(h_lo, c), chunk(x_res, c), col(norm, c), as_f32(chunk(h_hi, c)), MUL, SUB).then_inc(h_split, 1)
                dve.wait_ge(squared, q_index + 1)
                dve.wait_ge(summed, s_index + 1)
                V.tensor_tensor(sumsq[:, :], sumsq[:, :], sq[:, t, :], ADD).then_inc(summed, 1)

            def inverse(n):
                dve.wait_ge(root_done, n + 1)
                V.reciprocal(rms[:, :], rms[:, :]).then_inc(rms_ready, 1)
                dve.wait_ge(rms_ready, n + 1)

            clear_sums()
            dve.wait_ge(par_loaded, 16)
            for c in range(KD):
                dve.wait_ge(x_loaded[c // 2], 16)
                split_x(c, "mix0", H_IN + c, Q_IN + c, S_IN + c, c % 2)
                if c == 1:
                    for s in range(2):
                        split_unit(s, M_PW1, UNIT)
                if c == 5:
                    dve.wait_ge(tap_rounded, 1)
                    V.tensor_tensor(tap_lo[:, :], par[:, COL["w_dw"]:COL["w_dw"] + KD * TAPS], as_f32(tap_hi[:, :]), SUB).then_inc(taps_split, 1)
            inverse(0)
            dve.wait_ge(consts_set, CONSTS)

            steps_before = [sum(TAPS - n for n in PE_TAPS[:i]) for i in range(PW1_STEPS)]

            def taps(i, first=0, last=TAPS):
                for k in range(max(first, PE_TAPS[i]), last):
                    for t in range(2):
                        c = 2 * i + t
                        src, w = glu[:, t, k:k + T], col("w_dw", c * TAPS + k)
                        if k == PE_TAPS[i]:
                            V.tensor_scalar(conv_out[:, c, :], src, w, col("b_dw", c), MUL, ADD).then_inc(tap_step[t], 1)
                        else:
                            dve.wait_ge(tap_step[t], steps_before[i] + k - PE_TAPS[i])
                            V.scalar_tensor_tensor(conv_out[:, c, :], src, w, conv_out[:, c, :], MUL, ADD).then_inc(tap_step[t], 1)

            def conv_sum(i):
                for t in range(2):
                    dve.wait_ge(tap_step[t], steps_before[i] + TAPS - PE_TAPS[i])
                    dve.wait_ge(conv_mm[t], i + 1)
                    V.tensor_tensor(conv_out[:, 2 * i + t, :], bank[BANKS_CONV[i][t]][:, :], conv_out[:, 2 * i + t, :], ADD).then_inc(conv_drained, 1)

            for i in range(PW1_STEPS):
                if i:
                    taps(i - 1, last=EARLY_TAPS)
                    if i >= 2:
                        conv_sum(i - 2)
                    taps(i - 1, first=EARLY_TAPS)
                else:
                    split_unit(0, M_PW1 + 1, UNIT)
                for b, dst in ((2, gate), (0, val)):
                    for t in range(2):
                        dve.wait_ge(unit_done[b // 2], M_PW1 + i + 1)
                        V.tensor_tensor(dst[:, t, :], bank[b + t][:, :], rms[:, :], MUL).then_inc(drained[b + t], 1)
                for t in range(2):
                    dve.wait_ge(gate_ready[t], i + 1)
                    dve.wait_ge(drained[t], DRAINED_PW1 + i + 1)
                    if i:
                        dve.wait_ge(tap_step[t], steps_before[i - 1] + TAPS - PE_TAPS[i - 1])
                    V.scalar_tensor_tensor(glu[:, t, PAD:PAD + T], val[:, t, :], col("b_pw1", 2 * i + t), gate[:, t, :], ADD, MUL).then_inc(glu_done[t], 1)
                for s in range(2) if i else (1,):
                    split_unit(s, M_PW1 + i + 1, UNIT)
                for t in range(2):
                    dve.wait_ge(glu_rounded[t], i + 1)
                    slot = 2 * (i % 2) + t
                    V.tensor_tensor(glu_lo[:, slot, :], glu[:, t, :], as_f32(glu_hi[:, slot, :]), SUB).then_inc(glu_split[t], 1)
            taps(PW1_STEPS - 1, last=EARLY_TAPS)
            conv_sum(PW1_STEPS - 2)
            taps(PW1_STEPS - 1, first=EARLY_TAPS)
            conv_sum(PW1_STEPS - 1)

            dve.wait_ge(mean_ready, 1)
            for c in range(KD):
                V.tensor_tensor(conv_out[:, c, :], conv_out[:, c, :], mean[:, :], SUB).then_inc(centred, 1)
            clear_sums()
            dve.wait_ge(std_ready, 1)
            V.reciprocal(rstd[:, :], rstd[:, :]).then_inc(rstd_ready, 1)
            dve.wait_ge(rstd_ready, 1)

            def split_v(c):
                dve.wait_ge(v_rounded, c + 1)
                V.tensor_tensor(v_lo[:, c, :], conv_out[:, c, :], as_f32(v_hi[:, c, :]), SUB).then_inc(v_split, 1)

            for c in range(KD):
                V.tensor_tensor(conv_out[:, c, :], conv_out[:, c, :], rstd[:, :], MUL).then_inc(normed, 1)
                if c >= 2:
                    split_v(c - 2)
            split_v(KD - 2)
            split_v(KD - 1)

            for j in range(PW2_STEPS):
                for s in range(2):
                    for t in range(2):
                        c = 4 * j + 2 * s + t
                        dve.wait_ge(unit_done[s], M_PW2 + j + 1)
                        V.scalar_tensor_tensor(x_res[:, c, :], bank[2 * s + t][:, :], col("b_pw2", c), x_res[:, c, :], ADD, ADD).then_inc(x_updated, 1)
                    for t in range(2):
                        c = 4 * j + 2 * s + t
                        split_x(c, "ffn0", H_PW2 + c, Q_PW2 + c, S_PW2 + c, t)
                    split_unit(s, M_PW2 + j + 1, UNIT)

            def up_step(layer, i, columns):
                m = M_UP[layer]
                n = layer * UP_STEPS
                w = [COL["ffn_dw"] + 4 * (layer * KF + t) + 8 * i for t in range(2)]
                for t in range(2):
                    dve.wait_ge(unit_done[0], m + i + 1)
                    V.tensor_tensor(act_in[:, t, 2:2 + T], bank[t][:, :], rms[:, :], MUL).then_inc(drained[t], 1)
                split_unit(0, m + i + 1, columns)
                for t in range(2):
                    dve.wait_ge(tap2_done[t], n + i + 1)
                    V.scalar_tensor_tensor(y[:, t, :], act_in[:, t, 1:1 + T], par[:, bass.ds(w[t] + 1, 1)], y[:, t, :], MUL, ADD).then_inc(tap1_done[t], 1)
                for t in range(2):
                    dve.wait_ge(tap1_done[t], n + i + 1)
                    V.scalar_tensor_tensor(y[:, t, :], act_in[:, t, 0:T], par[:, bass.ds(w[t], 1)], y[:, t, :], MUL, ADD).then_inc(conv3_done[t], 1)
                for t in range(2):
                    dve.wait_ge(silu_done[t], n + i + 1)
                    V.tensor_tensor(y[:, t, :], y[:, t, :], rms[:, :], MUL).then_inc(act_scaled[t], 1)
                for t in range(2):
                    dve.wait_ge(act_scaled[t], n + i + 1)
                    dve.wait_ge(unit_done[1], m + i + 1)
                    V.tensor_tensor(y[:, t, :], bank[2 + t][:, :], y[:, t, :], MUL).then_inc(drained[2 + t], 1)
                for t in range(2):
                    dve.wait_ge(u_rounded[t], n + i + 1)
                    V.tensor_tensor(chunk(u_lo, 2 * i + t), y[:, t, :], as_f32(chunk(u_hi, 2 * i + t)), SUB).then_inc(u_split[t], 1)
                split_unit(1, m + i + 1, columns)

            def down_step(layer, j, columns):
                m = M_DOWN[layer]
                for t in range(2):
                    e = 2 * j + t
                    if columns[t]:
                        split_unit(0, m + e + 1, columns[t])
                    dve.wait_ge(unit_done[1], m + e + 1)
                    V.tensor_tensor(chunk(x_res, e), bank[t][:, :], chunk(x_res, e), ADD).then_inc(x_updated, 1)
                    split_x(e, None, None, Q_DOWN[layer] + e, S_DOWN[layer] + e, t)
                    if columns[t]:
                        split_unit(1, m + e + 1, columns[t])

            def split_pooled(c):
                dve.wait_ge(v_rounded, KD + c + 1)
                V.tensor_tensor(v_lo[:, c, :], pooled[:, c % 2, :], as_f32(v_hi[:, c, :]), SUB).then_inc(v_split, 1)

            for layer in range(DEPTH):
                if layer == 1:
                    inverse(2)
                    for buffer in (pool_h, win_a, win_b):
                        V.memset(buffer[:, :, 0:16], 0.0).then_inc(pool_step, 1)
                    steps = 3

                    for c in range(KD):
                        group, t = c // 2, c % 2
                        w = WINDOWS[group]
                        V.scalar_tensor_tensor(pool_h[:, t, 16:], x_res[:, c, :], col("mix1", c), rms[:, :], MUL, MUL).then_inc(pool_step, 1)
                        steps += 1
                        dve.wait_ge(pool_step, steps)
                        src, reach, dst = pool_h, 1, win_a
                        while reach < w:
                            V.tensor_tensor(dst[:, t, 16:], src[:, t, 16:], src[:, t, 16 - reach:16 - reach + T], ADD).then_inc(pool_step, 1)
                            steps += 1
                            dve.wait_ge(pool_step, steps)
                            src, dst = dst, (win_b if dst is win_a else win_a)
                            reach *= 2
                        V.tensor_tensor(dst[:, t, 16:16 + w - 1], src[:, t, 16:16 + w - 1], inv_count[:, 0:w - 1], MUL).then_inc(pool_step, 1)
                        steps += 1
                        dve.wait_ge(pool_step, steps)
                        if c >= 2:
                            dve.wait_ge(v_rounded, KD + c - 1)
                        V.tensor_tensor(pooled[:, t, 0:w - 1], dst[:, t, 16:16 + w - 1], pool_h[:, t, 16:16 + w - 1], SUB).then_inc(pool_step, 1)
                        V.scalar_tensor_tensor(pooled[:, t, w - 1:T], src[:, t, 16 + w - 1:16 + T], 1.0 / w, pool_h[:, t, 16 + w - 1:16 + T], MUL, SUB).then_inc(pooled_done, 1)
                        steps += 1
                        if c >= 1:
                            split_pooled(c - 1)
                    split_pooled(KD - 1)
                    clear_sums()
                    dve.wait_ge(v_split, 2 * KD)
                    for s in range(2):
                        for b in range(4):
                            e = 4 * s + b
                            dve.wait_ge(unit_done[s], M_POOL + 1)
                            V.tensor_scalar(pooled[:, b % 2, :], bank[b][:, :], col("pool_b", e), col("pool_s", e), ADD, MUL).then_inc(drained[b], 1)
                            dve.wait_ge(drained[b], DRAINED_POOL + s + 1)
                            V.tensor_tensor(x_res[:, e, :], pooled[:, b % 2, :], x_res[:, e, :], ADD).then_inc(x_updated, 1)
                            if b % 2:
                                for c in (e - 1, e):
                                    split_x(c, "ffn1", H_POOL + c, Q_POOL + c, S_POOL + c, c % 2)
                        split_unit(s, M_UP[1], UNIT)
                inverse(1 if layer == 0 else 3)
                with dve.Fori(0, UP_STEPS - 1) as i:
                    up_step(layer, i, UNIT)
                up_step(layer, UP_STEPS - 1, DOWN_UNIT)
                clear_sums()
                with dve.Fori(0, DOWN_STEPS // 2 - 1) as j:
                    down_step(layer, j, (DOWN_UNIT, DOWN_UNIT))
                down_step(layer, DOWN_STEPS // 2 - 1, (DOWN_UNIT, POOL_UNIT if layer == 0 else 0))
            inverse(4)
            for c in range(KD):
                V.scalar_tensor_tensor(out_sb[:, c, :], x_res[:, c, :], col("final", c), rms[:, :], MUL, MUL).then_inc(out_ready, 1)

        @block.tensor
        def _(pe):
            M = nc.tensor

            def three_passes(dst, s, w_at, hi, lo, start, stop):
                a, b = w_hi[s][:, w_at:w_at + P], w_lo[s][:, w_at:w_at + P]
                M.matmul(dst, a, hi, start=start, stop=False)
                M.matmul(dst, a, lo, start=False, stop=False)
                return M.matmul(dst, b, hi, start=False, stop=stop)

            def unit(s, m, hi, lo, before=None):
                pe.wait_ge(w_split[s], m + 1)
                for k in range(KD):
                    if before:
                        before(k)
                    for t in range(2):
                        last = three_passes(bank[2 * s + t][:, :], s, (2 * k + t) * P, hi[:, k, :], lo[:, k, :], k == 0, k == KD - 1)
                last.then_inc(unit_done[s], 1)

            def wait_drained(banks, count):
                for b in banks:
                    pe.wait_ge(drained[b], count)

            def sum_channels(n):
                pe.wait_ge(summed, (KD + 1) * (n + 1))
                M.matmul(bank[BANK_SUM][:, :], ones[:, :], sumsq[:, :], start=True, stop=True).then_inc(stat_mm, 1)

            def h_chunks(first):
                def before(k):
                    if k == 0 or k >= 6:
                        pe.wait_ge(h_split, first + max(k + 1, 6))
                return before

            def v_chunks(first):
                def before(k):
                    pe.wait_ge(v_split, first + k + 1)
                return before

            def tensor_taps(i):
                n = PE_TAPS[i]
                for t in range(2):
                    pe.wait_ge(diag_ready[t], 2 * sum(PE_TAPS[:i + 1]))
                    pe.wait_ge(glu_split[t], i + 1)
                    if 1 <= i < PW1_STEPS - 1:
                        pe.wait_ge(conv_drained, 2 * (i - 1) + t + 1)
                    for k in range(n):
                        slot, dst = 2 * (i % 2) + t, bank[BANKS_CONV[i][t]][:, :]
                        hi, lo = glu_hi[:, slot, k:k + T], glu_lo[:, slot, k:k + T]
                        M.matmul(dst, diag_hi[i % 2][t][:, k, :], hi, start=k == 0, stop=False)
                        M.matmul(dst, diag_hi[i % 2][t][:, k, :], lo, start=False, stop=False)
                        last = M.matmul(dst, diag_lo[i % 2][t][:, k, :], hi, start=False, stop=k == n - 1)
                    last.then_inc(conv_mm[t], 1)

            def sum_for_mean(i):
                for c in (2 * i, 2 * i + 1):
                    pe.wait_ge(conv_drained, c + 1)
                    last = M.matmul(bank[BANK_MEAN][:, :], ones[:, :], conv_out[:, c, :], start=c == 0, stop=c == KD - 1)
                if i == PW1_STEPS - 1:
                    last.then_inc(mean_mm, 1)

            pe.wait_ge(consts_set, CONSTS)
            for i in range(PW1_STEPS):
                for s in range(2):
                    if i:
                        wait_drained((2 * s, 2 * s + 1), DRAINED_PW1 + i)
                    unit(s, M_PW1 + i, h_hi, h_lo, (lambda k: pe.wait_ge(h_split, H_IN + k + 1)) if i == 0 and s == 0 else None)
                    if i == 0 and s == 0:
                        sum_channels(0)
                if i >= 2:
                    sum_for_mean(i - 2)
                if i:
                    tensor_taps(i - 1)
            tensor_taps(PW1_STEPS - 1)
            sum_for_mean(PW1_STEPS - 2)
            sum_for_mean(PW1_STEPS - 1)

            for c in range(KD):
                pe.wait_ge(dev_squared, c + 1)
                M.matmul(bank[BANK_SUM][:, :], ones[:, :], sq[:, c % 2, :], start=c == 0, stop=c == KD - 1).then_inc(dev_summed, 1)

            for j in range(PW2_STEPS):
                for s in range(2):
                    if j:
                        pe.wait_ge(x_updated, X_PW2 + 4 * (j - 1) + 2 * s + 2)
                    unit(s, M_PW2 + j, v_hi, v_lo, v_chunks(0) if j == 0 and s == 0 else None)

            def up_step(layer, i, norm=None):
                h = h_chunks(H_PW2 if layer == 0 else H_POOL)
                for s in range(2):
                    wait_drained((2 * s, 2 * s + 1), DRAINED_UP[layer] + i)
                    unit(s, M_UP[layer] + i, h_hi, h_lo, h)
                    if s == 0 and norm is not None:
                        sum_channels(norm)

            def down_step(layer, j):
                for t in range(2):
                    e = 2 * j + t
                    pe.wait_ge(drained[t], DRAINED_UP[layer] + UP_STEPS)
                    pe.wait_ge(x_updated, X_DOWN[layer] + e - 1)
                    for s in range(2):
                        pe.wait_ge(w_split[s], M_DOWN[layer] + e + 1)
                        for b in range(2):
                            pe.wait_ge(u_split[b], UP_STEPS * layer + ((DOWN_K + 1) // 2 if s == 0 else UP_STEPS))
                        for k in range(DOWN_K):
                            kk = s * DOWN_K + k
                            last = three_passes(bank[t][:, :], s, k * P, u_hi[:, kk, :], u_lo[:, kk, :], kk == 0, kk == KF - 1)
                        last.then_inc(unit_done[s], 1)

            for layer in range(DEPTH):
                if layer == 1:
                    sum_channels(2)
                    for s in range(2):
                        pe.wait_ge(w_split[s], M_POOL + 1)
                        for b in range(4):
                            if s:
                                wait_drained((b,), DRAINED_POOL + s)
                            group = 2 * s + b // 2
                            pe.wait_ge(v_split, KD + 2 * group + 2)
                            for k in range(2):
                                c = 2 * group + k
                                last = three_passes(bank[b][:, :], s, ((b // 2) * 2 + k) * 2 * P + (b % 2) * P, v_hi[:, c, :], v_lo[:, c, :], k == 0, k == 1)
                        last.then_inc(unit_done[s], 1)
                up_step(layer, 0, norm=1 if layer == 0 else 3)
                with pe.Fori(1, UP_STEPS) as i:
                    up_step(layer, i)
                with pe.Fori(0, DOWN_STEPS // 2) as j:
                    down_step(layer, j)
            sum_channels(4)


def _columns(v):
    return v.reshape(-1, P).T


def kernel(**inputs):
    import numpy as np
    import concourse.bacc as bacc
    from concourse.bass_utils import run_bass_kernel_spmd

    a = {k: np.asarray(v) for k, v in inputs.items()}
    w_dw = a["conv_w_dw"][0].reshape(TAPS, KD, P).transpose(2, 1, 0).reshape(P, KD * TAPS)
    ffn_dw = np.concatenate([a["ffn_w_dw"], a["ffn_b_dw"][:, None, :]], axis=1)
    ffn_dw = ffn_dw.reshape(DEPTH, 4, KF, P).transpose(3, 0, 2, 1).reshape(P, DEPTH * KF * 4)
    vecs = np.concatenate(
        [_columns(v) for v in (a["norm_mix"][0], a["norm_mix"][1], a["norm_ffn"][0], a["norm_ffn"][1], a["final_norm"],
                               a["conv_b_pw1"][0], a["conv_b_dw"][0], a["conv_ln_g"][0], a["conv_ln_b"][0],
                               a["conv_b_pw2"][0], a["pool_b"][0], a["pool_scale"][0])] + [w_dw, ffn_dw], axis=1)

    pw1 = a["conv_w_pw1"][0].reshape(KD, P, 2, PW1_STEPS, 2 * P).transpose(3, 2, 1, 0, 4).reshape(2 * PW1_STEPS, P, UNIT)
    pw2 = a["conv_w_pw2"][0].reshape(KD, P, 2 * PW2_STEPS, 2 * P).transpose(2, 1, 0, 3).reshape(2 * PW2_STEPS, P, UNIT)
    up = a["ffn_w_up"].reshape(DEPTH, KD, P, 2, UP_STEPS, 2 * P).transpose(0, 4, 3, 2, 1, 5).reshape(DEPTH * 2 * UP_STEPS, P, UNIT)
    down = a["ffn_w_down"].reshape(DEPTH, 2, DOWN_K, P, DOWN_STEPS, P).transpose(0, 4, 1, 3, 2, 5).reshape(DEPTH * 2 * DOWN_STEPS, P, DOWN_UNIT)
    pool = a["pool_w"][0].reshape(2, 2, 2, P, 2 * P).transpose(0, 3, 1, 2, 4).reshape(2, P, POOL_UNIT)

    arrays = {
        "x": a["x"][0].reshape(T, KD, P).transpose(2, 1, 0),
        "vecs": vecs,
        "ident": np.eye(P, dtype=np.float32),
        "w_pw1": pw1, "w_pw2": pw2, "w_up": up, "w_down": down, "w_pool": pool,
    }
    arrays = {k: np.ascontiguousarray(v) for k, v in arrays.items()}
    nc = bacc.Bacc("TRN2", target_bir_lowering=False, num_devices=1)
    args = [nc.dram_tensor(k, v.shape, mybir.dt.float32, kind="ExternalInput").ap() for k, v in arrays.items()]
    out = nc.dram_tensor("out", (P, KD, T), mybir.dt.float32, kind="ExternalOutput").ap()
    build(nc, *args, out)
    r = run_bass_kernel_spmd(nc, [arrays], core_ids=[0])
    return np.ascontiguousarray(r.results[0]["out"].transpose(2, 1, 0).reshape(1, T, D))
```

```python
import concourse.bass as bass
from concourse import mybir
from contextlib import ExitStack

P = 128
D = 1024
T = 512
FF = 2816
KD = D // P
KF = FF // P
UNIT = 8 * 2 * P
DOWN_K = KF // 2
DOWN_UNIT = DOWN_K * P
POOL_UNIT = 2 * 2 * 2 * P
TAPS = 31
PAD = TAPS - 1
WINDOWS = (2, 4, 8, 16)
GROUP = D // len(WINDOWS)
BLOCKS = T // P
BAND = 3 * P
START = 16
BAND_COLS = len(WINDOWS) * (BAND + START)
RMS_EPS = 1e-6
LN_EPS = 1e-5
DEPTH = 2

PW1_STEPS = 4
PW2_STEPS = 2
UP_STEPS = KF // 2
DOWN_STEPS = KD
M_PW1 = 0
M_PW2 = M_PW1 + PW1_STEPS
M_UP = [M_PW2 + PW2_STEPS, 0]
M_DOWN = [M_UP[0] + UP_STEPS, 0]
M_POOL = M_DOWN[0] + DOWN_STEPS
M_UP[1] = M_POOL + 1
M_DOWN[1] = M_UP[1] + UP_STEPS
DRAINED_PW1, DRAINED_UP = 0, (PW1_STEPS, PW1_STEPS + UP_STEPS)
X_PW2, X_DOWN, X_POOL = 0, (KD, 3 * KD), 2 * KD
H_IN, H_PW2, H_DOWN, H_POOL = 0, KD, 2 * KD, 3 * KD
Q_IN, Q_PW2, Q_DOWN, Q_POOL = 0, KD, (2 * KD, 4 * KD), 3 * KD
S_IN, S_PW2, S_DOWN, S_POOL = 0, KD + 1, (2 * (KD + 1), 4 * (KD + 1)), 3 * (KD + 1)

COL = {}
_at = 0
for _name, _n in [("mix0", KD), ("mix1", KD), ("ffn0", KD), ("ffn1", KD), ("final", KD), ("b_pw1", 2 * KD),
                  ("b_dw", KD), ("ln_g", KD), ("ln_b", KD), ("b_pw2", KD), ("pool_b", KD), ("pool_s", KD),
                  ("w_dw", KD * TAPS), ("ffn_dw", DEPTH * KF * 4)]:
    COL[_name] = _at
    _at += _n
N_COLS = _at

PE_TAPS = [12, 12, 12, 12]
DIAG_TAPS = [max(PE_TAPS[0::2]), max(PE_TAPS[1::2])]

EARLY_TAPS = 22

BANK_SUM, BANK_MEAN = 4, 7
BANKS_CONV = [(5, 6), (5, 6), (5, 6), (0, 1)]
BANKS_MAP = [(2, 3), (5, 6), (7, 0), (2, 3)]
BANKS_WINDOW = (4, 1, 5, 6, 7, 4, 5, 6)


def build(nc, x_in, vecs, ident_in, band_in, w_pw1, w_pw2, w_up, w_down, w_pool, out):
    f32, f32r = mybir.dt.float32, mybir.dt.float32r
    ALU, ACT = mybir.AluOpType, mybir.ActivationFunctionType
    MUL, ADD, SUB = ALU.mult, ALU.add, ALU.subtract

    ctx = ExitStack()
    with ctx:
        at = [nc.sbuf_base]

        def place(name, shape, dt, offset=None):
            size = 4
            for n in shape[1:]:
                size *= n
            size = (size + 31) // 32 * 32
            if offset is None:
                offset = at[0]
                at[0] += size
            return nc.alloc_sbuf_tensor_at(name, shape, dt, offset=offset)

        at[0] = (at[0] + 31) // 32 * 32
        par = place("par", [P, N_COLS], f32)
        ident = place("ident", [P, P], f32)
        ones = place("ones", [P, P], f32)
        eps = place("eps", [P, 2], f32)
        inv_count = place("inv_count", [P, 16], f32)
        root_tok = place("root_tok", [P, BLOCKS], f32)
        pool_gain = place("pool_gain", [P, KD], f32)
        pool_shift = place("pool_shift", [P, KD], f32)
        start_sum = place("start_sum", [P, START], f32)
        x_res = place("x_res", [P, KD, T], f32)
        h_hi = place("h_hi", [P, KD, T], f32r)
        h_lo = place("h_lo", [P, KD, T], f32r)
        w_raw = [place(f"w_raw{s}", [P, UNIT], f32) for s in range(2)]
        w_hi = [place(f"w_hi{s}", [P, UNIT], f32r) for s in range(2)]
        w_lo = [place(f"w_lo{s}", [P, UNIT], f32r) for s in range(2)]
        rms = place("rms", [P, T], f32)
        sumsq = place("sumsq", [P, T], f32)
        sq = place("sq", [P, 2, T], f32)
        ACT_IN = at[0]
        act_in = place("act_in", [P, 2, 2 + T], f32)
        y = place("y", [P, 2, T], f32)
        U_HI = at[0]
        u_hi = place("u_hi", [P, KF, T], f32r)
        U_LO = at[0]
        u_lo = place("u_lo", [P, KF, T], f32r)
        v_hi, v_lo = u_lo[:, 0:KD, :], u_lo[:, KD:2 * KD, :]
        conv_out = place("conv_out", [P, KD, T], f32, U_HI)
        o = U_HI + KD * T * 4
        glu = place("glu", [P, 2, PAD + T], f32, o)
        glu_hi = place("glu_hi", [P, 4, PAD + T], f32r, o + 4352)
        glu_lo = place("glu_lo", [P, 4, PAD + T], f32r, o + 4352 + 8704)
        val, gate = y, act_in[:, :, 2:2 + T]
        o_taps = o + 5 * 4352
        tap_hi = place("tap_hi", [P, KD * TAPS], f32r, o_taps)
        tap_lo = place("tap_lo", [P, KD * TAPS], f32r, o_taps + 1024)
        o_diag = [o_taps + 2048, o_taps + 2048 + 4 * DIAG_TAPS[0] * P * 4]
        diag_hi = [[place(f"diag_hi{q}{t}", [P, DIAG_TAPS[q], P], f32r, o_diag[q] + t * DIAG_TAPS[q] * P * 4)
                    for t in range(2)] for q in range(2)]
        diag_lo = [[place(f"diag_lo{q}{t}", [P, DIAG_TAPS[q], P], f32r, o_diag[q] + (2 + t) * DIAG_TAPS[q] * P * 4)
                    for t in range(2)] for q in range(2)]
        assert o_diag[1] + 4 * DIAG_TAPS[1] * P * 4 <= U_HI + 2 * KF * T * 4
        mean = place("mean", [P, T], f32, o)
        rstd = place("rstd", [P, T], f32, o + 2048)
        band_raw = place("band_raw", [P, BAND_COLS], f32, ACT_IN)
        band = place("band", [P, BAND_COLS], f32r, ACT_IN)
        map_hi = place("map_hi", [P, BLOCKS, D], f32r, U_HI)
        map_lo = place("map_lo", [P, BLOCKS, D], f32r, U_HI + BLOCKS * D * 4)
        pool_sq = place("pool_sq", [P, KD, T], f32, U_HI + 2 * BLOCKS * D * 4)
        out_sb = place("out_sb", [P, KD, T], f32, U_HI)

        bank = [ctx.enter_context(nc.psum_tensor(f"bank{b}", [P, T], f32)) for b in range(8)]

        def sem(name):
            return ctx.enter_context(nc.semaphore(name))

        def sems(name, n=2):
            return [sem(f"{name}{i}") for i in range(n)]

        par_loaded, ident_loaded, out_stored = sem("par_loaded"), sem("ident_loaded"), sem("out_stored")
        x_loaded = sems("x_loaded", 4)
        raw_loaded = sems("raw_loaded")
        w_rounded = sems("w_rounded")
        w_split = sems("w_split")
        unit_done = sems("unit_done")
        drained = sems("drained", 4)
        x_updated, h_rounded, h_split = sem("x_updated"), sem("h_rounded"), sem("h_split")
        squared, summed = sem("squared"), sem("summed")
        stat_mm, root_done, rms_ready = sem("stat_mm"), sem("root_done"), sem("rms_ready")
        consts_set, memory_cleared = sem("consts_set"), sem("memory_cleared")
        taps_split, tap_rounded = sem("taps_split"), sem("tap_rounded")
        diag_ready = sems("diag_ready")
        gate_ready, glu_done = sems("gate_ready"), sems("glu_done")
        glu_rounded, glu_split = sems("glu_rounded"), sems("glu_split")
        tap_step = sems("tap_step")
        conv_mm, conv_drained = sems("conv_mm"), sem("conv_drained")
        mean_mm, mean_ready, centred = sem("mean_mm"), sem("mean_ready"), sem("centred")
        dev_squared, dev_summed = sem("dev_squared"), sem("dev_summed")
        std_ready, rstd_ready = sem("std_ready"), sem("rstd_ready")
        normed, swished, v_rounded, v_split = sem("normed"), sem("swished"), sem("v_rounded"), sem("v_split")
        tap2_done, tap1_done, conv3_done = sems("tap2_done"), sems("tap1_done"), sems("conv3_done")
        silu_done, act_scaled = sems("silu_done"), sems("act_scaled")
        u_rounded, u_split = sems("u_rounded"), sems("u_split")
        band_loaded, band_rounded, pool_vecs = sem("band_loaded"), sem("band_rounded"), sem("pool_vecs")
        shifted = sem("shifted")
        map_mm, map_rounded, map_split = sem("map_mm"), sem("map_rounded"), sem("map_split")
        window_mm, start_scaled, start_added = sem("window_mm"), sem("start_scaled"), sem("start_added")
        out_ready = sem("out_ready")

        def col(name, i, n=1):
            return par[:, bass.ds(COL[name] + i, n)]

        def flat(ap):
            return ap.rearrange("p a t -> p (a t)")

        def chunk(tensor, c):
            return flat(tensor[:, bass.ds(c, 1), :])

        def as_f32(ap):
            return ap.bitcast(f32)

        def map_bank(group, j):
            return bank[BANKS_MAP[group][j // 2]][:, (j % 2) * GROUP:(j % 2 + 1) * GROUP]

        block = ctx.enter_context(nc.Block())

        @block.sync
        def _(sp):
            sp.dma_start(par[:, :], vecs).then_inc(par_loaded, 16)
            sp.dma_start(x_res[:, 0:2, :], x_in[:, 0:2, :]).then_inc(x_loaded[0], 16)

            def load_step(source, first, m, columns, wait=True):
                for s in range(2):
                    if wait:
                        sp.wait_ge(w_split[s], m)
                    sp.dma_start(w_raw[s][:, 0:columns], source[first + s]).then_inc(raw_loaded[s], 16)

            load_step(w_pw1, 0, M_PW1, UNIT, wait=False)
            for q in range(1, 4):
                sp.dma_start(x_res[:, 2 * q:2 * q + 2, :], x_in[:, 2 * q:2 * q + 2, :]).then_inc(x_loaded[q], 16)
            sp.dma_start(ident[:, :], ident_in).then_inc(ident_loaded, 16)
            with sp.Fori(1, PW1_STEPS) as i:
                load_step(w_pw1, 2 * i, M_PW1 + i, UNIT)
            with sp.Fori(0, PW2_STEPS) as i:
                load_step(w_pw2, 2 * i, M_PW2 + i, UNIT)
            for layer in range(DEPTH):
                if layer == 1:
                    for t in range(2):
                        sp.wait_ge(u_split[t], UP_STEPS)
                    sp.dma_start(band_raw[:, :], band_in).then_inc(band_loaded, 16)
                    load_step(w_pool, 0, M_POOL, POOL_UNIT)
                with sp.Fori(0, UP_STEPS) as i:
                    load_step(w_up, 2 * i + 2 * UP_STEPS * layer, M_UP[layer] + i, UNIT)
                with sp.Fori(0, DOWN_STEPS) as e:
                    load_step(w_down, 2 * e + 2 * DOWN_STEPS * layer, M_DOWN[layer] + e, DOWN_UNIT)
            for c in range(KD):
                sp.wait_ge(out_ready, c + 1)
                sp.dma_start(out[:, c, :], out_sb[:, c, :]).then_inc(out_stored, 16)
            sp.wait_ge(out_stored, 16 * KD)

        @block.gpsimd
        def _(pool):
            nc.gpsimd.memset(ones[:, :], 1.0).then_inc(consts_set, 1)
            nc.gpsimd.memset(eps[:, 0:1], RMS_EPS).then_inc(consts_set, 1)
            nc.gpsimd.memset(eps[:, 1:2], LN_EPS).then_inc(consts_set, 1)
            nc.gpsimd.memset(act_in[:, :, 0:2], 0.0).then_inc(consts_set, 1)
            nc.gpsimd.memset(glu[:, :, 0:PAD], 0.0).then_inc(consts_set, 1)
            for t in range(max(WINDOWS) - 1):
                nc.gpsimd.memset(inv_count[:, t:t + 1], 1.0 / (t + 1)).then_inc(consts_set, 1)

        CONSTS = 5 + max(WINDOWS) - 1

        @block.scalar
        def _(act):
            def round_unit(s, m, columns, first=False):
                act.wait_ge(raw_loaded[s], 16 * (m + 1))
                if not first:
                    act.wait_ge(unit_done[s], m)
                nc.scalar.activation(w_hi[s][:, 0:columns], w_raw[s][:, 0:columns], ACT.Copy).then_inc(w_rounded[s], 1)

            def round_x(c, norm, s_index, t):
                act.wait_ge(summed, s_index)
                nc.scalar.activation(sq[:, t, :], chunk(x_res, c), ACT.Square).then_inc(squared, 1)
                if norm is not None:
                    nc.scalar.activation(chunk(h_hi, c), chunk(x_res, c), ACT.Copy, scale=col(norm, c)).then_inc(h_rounded, 1)

            def root(n):
                act.wait_ge(stat_mm, n + 1)
                nc.scalar.activation(rms[:, :], bank[BANK_SUM][:, :], ACT.Sqrt, scale=1.0 / D, bias=eps[:, 0:1]).then_inc(root_done, 1)

            act.wait_ge(par_loaded, 16)
            act.wait_ge(consts_set, CONSTS)
            for c in range(KD):
                act.wait_ge(x_loaded[c // 2], 16)
                round_x(c, "mix0", S_IN + max(c, 1), c % 2)
                if c == 1:
                    for s in range(2):
                        round_unit(s, M_PW1, UNIT, first=True)
                if c == 5:
                    nc.scalar.activation(tap_hi[:, :], par[:, COL["w_dw"]:COL["w_dw"] + KD * TAPS], ACT.Copy).then_inc(tap_rounded, 1)
            root(0)

            def diagonals(i, t):
                if i == 0 and t == 0:
                    act.wait_ge(ident_loaded, 16)
                    act.wait_ge(taps_split, 1)
                if i >= 2:
                    act.wait_ge(conv_mm[t], i - 1)
                for k in range(PE_TAPS[i]):
                    w = (2 * i + t) * TAPS + k
                    nc.scalar.activation(diag_hi[i % 2][t][:, k, :], ident[:, :], ACT.Copy, scale=as_f32(tap_hi[:, w:w + 1])).then_inc(diag_ready[t], 1)
                    nc.scalar.activation(diag_lo[i % 2][t][:, k, :], ident[:, :], ACT.Copy, scale=as_f32(tap_lo[:, w:w + 1])).then_inc(diag_ready[t], 1)

            for i in range(PW1_STEPS):
                if i == 0:
                    round_unit(0, M_PW1 + 1, UNIT)
                for t in range(2):
                    act.wait_ge(drained[2 + t], DRAINED_PW1 + i + 1)
                    nc.scalar.activation(gate[:, t, :], gate[:, t, :], ACT.Sigmoid, bias=col("b_pw1", KD + 2 * i + t)).then_inc(gate_ready[t], 1)
                if i:
                    round_unit(0, M_PW1 + i + 1, UNIT)
                round_unit(1, M_PW1 + i + 1, UNIT)
                for t in range(2):
                    act.wait_ge(glu_done[t], i + 1)
                    if i >= 2:
                        act.wait_ge(conv_mm[t], i - 1)
                    nc.scalar.activation(glu_hi[:, 2 * (i % 2) + t, :], glu[:, t, :], ACT.Copy).then_inc(glu_rounded[t], 1)
                for pair in ((0, 1) if i == 0 else (i + 1,) if i < PW1_STEPS - 1 else ()):
                    for t in range(2):
                        diagonals(pair, t)

            act.wait_ge(mean_mm, 1)
            nc.scalar.activation(mean[:, :], bank[BANK_MEAN][:, :], ACT.Copy, scale=1.0 / D).then_inc(mean_ready, 1)
            for c in range(KD):
                act.wait_ge(centred, c + 1)
                if c >= 2:
                    act.wait_ge(dev_summed, c - 1)
                nc.scalar.activation(sq[:, c % 2, :], conv_out[:, c, :], ACT.Square).then_inc(dev_squared, 1)
            act.wait_ge(dev_summed, KD)
            nc.scalar.activation(rstd[:, :], bank[BANK_SUM][:, :], ACT.Sqrt, scale=1.0 / D, bias=eps[:, 1:2]).then_inc(std_ready, 1)
            for c in range(KD):
                act.wait_ge(normed, c + 1)
                nc.scalar.activation(conv_out[:, c, :], conv_out[:, c, :], ACT.Silu, scale=col("ln_g", c), bias=col("ln_b", c)).then_inc(swished, 1)
                act.wait_ge(swished, c + 1)
                nc.scalar.activation(v_hi[:, c, :], conv_out[:, c, :], ACT.Copy).then_inc(v_rounded, 1)

            def pw2_step(j, next_m):
                for s in range(2):
                    for t in range(2):
                        c = 4 * j + 2 * s + t
                        act.wait_ge(x_updated, X_PW2 + c + 1)
                        round_x(c, "ffn0", S_PW2 + c, t)
                    round_unit(s, next_m, UNIT)

            for j in range(PW2_STEPS):
                pw2_step(j, M_PW2 + j + 1)

            def up_step(layer, i, columns):
                m, f = M_UP[layer], DRAINED_UP[layer]
                n = layer * UP_STEPS
                for t in range(2):
                    act.wait_ge(drained[t], f + i + 1)
                    w = COL["ffn_dw"] + 4 * (layer * KF + t) + 8 * i
                    nc.scalar.activation(y[:, t, :], act_in[:, t, 2:2 + T], ACT.Identity,
                                         scale=par[:, bass.ds(w + 2, 1)], bias=par[:, bass.ds(w + 3, 1)]).then_inc(tap2_done[t], 1)
                round_unit(0, m + i + 1, columns)
                for t in range(2):
                    act.wait_ge(conv3_done[t], n + i + 1)
                    nc.scalar.activation(y[:, t, :], y[:, t, :], ACT.Silu).then_inc(silu_done[t], 1)
                for t in range(2):
                    act.wait_ge(drained[2 + t], f + i + 1)
                    nc.scalar.activation(chunk(u_hi, 2 * i + t), y[:, t, :], ACT.Copy).then_inc(u_rounded[t], 1)
                round_unit(1, m + i + 1, columns)

            def down_step(layer, j, columns):
                m = M_DOWN[layer]
                for t in range(2):
                    round_unit(0, m + 2 * j + t + 1, columns[t])
                    act.wait_ge(x_updated, X_DOWN[layer] + 2 * j + t + 1)
                    round_x(2 * j + t, "mix1" if layer == 0 else None, S_DOWN[layer] + 2 * j + t, t)
                    round_unit(1, m + 2 * j + t + 1, columns[t])

            for layer in range(DEPTH):
                if layer == 1:
                    act.wait_ge(band_loaded, 16)
                    nc.scalar.activation(band[:, :], band_raw[:, :], ACT.Copy).then_inc(band_rounded, 1)
                    act.wait_ge(stat_mm, 3)
                    nc.scalar.activation(root_tok[:, :], bank[BANK_SUM][:, 0:BLOCKS], ACT.Sqrt, scale=1.0 / D, bias=eps[:, 0:1]).then_inc(root_done, 1)
                    act.wait_ge(rms_ready, 3)
                    for group in range(len(WINDOWS)):
                        if group == 3:
                            round_unit(0, M_UP[1], UNIT)
                        for j in range(BLOCKS):
                            act.wait_ge(map_mm, BLOCKS * group + j // 2 * 2 + 2)
                            nc.scalar.activation(map_hi[:, j, group * GROUP:(group + 1) * GROUP], map_bank(group, j), ACT.Copy, scale=root_tok[:, j:j + 1]).then_inc(map_rounded, 1)
                    for c in range(KD):
                        act.wait_ge(x_updated, X_POOL + c + 1)
                        nc.scalar.activation(h_hi[:, c, :], x_res[:, c, :], ACT.Copy, scale=col("ffn1", c)).then_inc(h_rounded, 1)
                        nc.scalar.activation(pool_sq[:, c, :], x_res[:, c, :], ACT.Square).then_inc(squared, 1)
                        if c == 5:
                            round_unit(1, M_UP[1], UNIT)
                root(1 if layer == 0 else 3)
                with act.Fori(0, UP_STEPS - 1) as i:
                    up_step(layer, i, UNIT)
                up_step(layer, UP_STEPS - 1, DOWN_UNIT)
                with act.Fori(0, DOWN_STEPS // 2 - 1) as j:
                    down_step(layer, j, (DOWN_UNIT, DOWN_UNIT))
                j = DOWN_STEPS // 2 - 1
                if layer == 0:
                    down_step(layer, j, (DOWN_UNIT, POOL_UNIT))
                else:
                    m = M_DOWN[1] + 2 * j + 1
                    for t in range(2):
                        if t == 0:
                            round_unit(0, m, DOWN_UNIT)
                        act.wait_ge(x_updated, X_DOWN[1] + 2 * j + t + 1)
                        round_x(2 * j + t, None, S_DOWN[1] + 2 * j + t, t)
                        if t == 0:
                            round_unit(1, m, DOWN_UNIT)
            root(4)

        @block.vector
        def _(dve):
            V = nc.vector

            def split_unit(s, m, columns):
                dve.wait_ge(w_rounded[s], m + 1)
                V.tensor_tensor(w_lo[s][:, 0:columns], w_raw[s][:, 0:columns], as_f32(w_hi[s][:, 0:columns]), SUB).then_inc(w_split[s], 1)

            def clear_sums():
                V.memset(sumsq[:, :], 0.0).then_inc(summed, 1)

            def split_x(c, norm, h_index, q_index, s_index, t):
                if norm is not None:
                    dve.wait_ge(h_rounded, h_index + 1)
                    V.scalar_tensor_tensor(chunk(h_lo, c), chunk(x_res, c), col(norm, c), as_f32(chunk(h_hi, c)), MUL, SUB).then_inc(h_split, 1)
                dve.wait_ge(squared, q_index + 1)
                dve.wait_ge(summed, s_index + 1)
                V.tensor_tensor(sumsq[:, :], sumsq[:, :], sq[:, t, :], ADD).then_inc(summed, 1)

            def inverse(n):
                dve.wait_ge(root_done, n + 1)
                V.reciprocal(rms[:, :], rms[:, :]).then_inc(rms_ready, 1)
                dve.wait_ge(rms_ready, n + 1)

            clear_sums()
            dve.wait_ge(par_loaded, 16)
            for c in range(KD):
                dve.wait_ge(x_loaded[c // 2], 16)
                split_x(c, "mix0", H_IN + c, Q_IN + c, S_IN + c, c % 2)
                if c == 1:
                    for s in range(2):
                        split_unit(s, M_PW1, UNIT)
                if c == 5:
                    dve.wait_ge(tap_rounded, 1)
                    V.tensor_tensor(tap_lo[:, :], par[:, COL["w_dw"]:COL["w_dw"] + KD * TAPS], as_f32(tap_hi[:, :]), SUB).then_inc(taps_split, 1)
            inverse(0)
            dve.wait_ge(consts_set, CONSTS)
            V.tensor_tensor(pool_shift[:, :], col("pool_b", 0, KD), col("pool_s", 0, KD), MUL).then_inc(pool_vecs, 1)
            for group, w in enumerate(WINDOWS):
                V.tensor_scalar(pool_gain[:, 2 * group:2 * group + 2], col("pool_s", 2 * group, 2), 1.0 / w, None, MUL).then_inc(pool_vecs, 1)

            steps_before = [sum(TAPS - n for n in PE_TAPS[:i]) for i in range(PW1_STEPS)]

            def taps(i, first=0, last=TAPS):
                for k in range(max(first, PE_TAPS[i]), last):
                    for t in range(2):
                        c = 2 * i + t
                        src, w = glu[:, t, k:k + T], col("w_dw", c * TAPS + k)
                        if k == PE_TAPS[i]:
                            V.tensor_scalar(conv_out[:, c, :], src, w, col("b_dw", c), MUL, ADD).then_inc(tap_step[t], 1)
                        else:
                            dve.wait_ge(tap_step[t], steps_before[i] + k - PE_TAPS[i])
                            V.scalar_tensor_tensor(conv_out[:, c, :], src, w, conv_out[:, c, :], MUL, ADD).then_inc(tap_step[t], 1)

            def conv_sum(i):
                for t in range(2):
                    dve.wait_ge(tap_step[t], steps_before[i] + TAPS - PE_TAPS[i])
                    dve.wait_ge(conv_mm[t], i + 1)
                    V.tensor_tensor(conv_out[:, 2 * i + t, :], bank[BANKS_CONV[i][t]][:, :], conv_out[:, 2 * i + t, :], ADD).then_inc(conv_drained, 1)

            for i in range(PW1_STEPS):
                if i:
                    taps(i - 1, last=EARLY_TAPS)
                    if i >= 2:
                        conv_sum(i - 2)
                    taps(i - 1, first=EARLY_TAPS)
                else:
                    split_unit(0, M_PW1 + 1, UNIT)
                for b, dst in ((2, gate), (0, val)):
                    for t in range(2):
                        dve.wait_ge(unit_done[b // 2], M_PW1 + i + 1)
                        V.tensor_tensor(dst[:, t, :], bank[b + t][:, :], rms[:, :], MUL).then_inc(drained[b + t], 1)
                for t in range(2):
                    dve.wait_ge(gate_ready[t], i + 1)
                    dve.wait_ge(drained[t], DRAINED_PW1 + i + 1)
                    if i:
                        dve.wait_ge(tap_step[t], steps_before[i - 1] + TAPS - PE_TAPS[i - 1])
                    V.scalar_tensor_tensor(glu[:, t, PAD:PAD + T], val[:, t, :], col("b_pw1", 2 * i + t), gate[:, t, :], ADD, MUL).then_inc(glu_done[t], 1)
                for s in range(2) if i else (1,):
                    split_unit(s, M_PW1 + i + 1, UNIT)
                for t in range(2):
                    dve.wait_ge(glu_rounded[t], i + 1)
                    slot = 2 * (i % 2) + t
                    V.tensor_tensor(glu_lo[:, slot, :], glu[:, t, :], as_f32(glu_hi[:, slot, :]), SUB).then_inc(glu_split[t], 1)
            taps(PW1_STEPS - 1, last=EARLY_TAPS)
            conv_sum(PW1_STEPS - 2)
            taps(PW1_STEPS - 1, first=EARLY_TAPS)
            conv_sum(PW1_STEPS - 1)

            dve.wait_ge(mean_ready, 1)
            for c in range(KD):
                V.tensor_tensor(conv_out[:, c, :], conv_out[:, c, :], mean[:, :], SUB).then_inc(centred, 1)
            clear_sums()
            dve.wait_ge(std_ready, 1)
            V.reciprocal(rstd[:, :], rstd[:, :]).then_inc(rstd_ready, 1)
            dve.wait_ge(rstd_ready, 1)

            def split_v(c):
                dve.wait_ge(v_rounded, c + 1)
                V.tensor_tensor(v_lo[:, c, :], conv_out[:, c, :], as_f32(v_hi[:, c, :]), SUB).then_inc(v_split, 1)

            for c in range(KD):
                V.tensor_tensor(conv_out[:, c, :], conv_out[:, c, :], rstd[:, :], MUL).then_inc(normed, 1)
                if c >= 2:
                    split_v(c - 2)
            split_v(KD - 2)
            split_v(KD - 1)

            for j in range(PW2_STEPS):
                for s in range(2):
                    for t in range(2):
                        c = 4 * j + 2 * s + t
                        dve.wait_ge(unit_done[s], M_PW2 + j + 1)
                        V.scalar_tensor_tensor(x_res[:, c, :], bank[2 * s + t][:, :], col("b_pw2", c), x_res[:, c, :], ADD, ADD).then_inc(x_updated, 1)
                    for t in range(2):
                        c = 4 * j + 2 * s + t
                        split_x(c, "ffn0", H_PW2 + c, Q_PW2 + c, S_PW2 + c, t)
                    split_unit(s, M_PW2 + j + 1, UNIT)

            def up_step(layer, i, columns):
                m = M_UP[layer]
                n = layer * UP_STEPS
                w = [COL["ffn_dw"] + 4 * (layer * KF + t) + 8 * i for t in range(2)]
                for t in range(2):
                    dve.wait_ge(unit_done[0], m + i + 1)
                    V.tensor_tensor(act_in[:, t, 2:2 + T], bank[t][:, :], rms[:, :], MUL).then_inc(drained[t], 1)
                split_unit(0, m + i + 1, columns)
                for t in range(2):
                    dve.wait_ge(tap2_done[t], n + i + 1)
                    V.scalar_tensor_tensor(y[:, t, :], act_in[:, t, 1:1 + T], par[:, bass.ds(w[t] + 1, 1)], y[:, t, :], MUL, ADD).then_inc(tap1_done[t], 1)
                for t in range(2):
                    dve.wait_ge(tap1_done[t], n + i + 1)
                    V.scalar_tensor_tensor(y[:, t, :], act_in[:, t, 0:T], par[:, bass.ds(w[t], 1)], y[:, t, :], MUL, ADD).then_inc(conv3_done[t], 1)
                for t in range(2):
                    dve.wait_ge(silu_done[t], n + i + 1)
                    V.tensor_tensor(y[:, t, :], y[:, t, :], rms[:, :], MUL).then_inc(act_scaled[t], 1)
                for t in range(2):
                    dve.wait_ge(act_scaled[t], n + i + 1)
                    dve.wait_ge(unit_done[1], m + i + 1)
                    V.tensor_tensor(y[:, t, :], bank[2 + t][:, :], y[:, t, :], MUL).then_inc(drained[2 + t], 1)
                for t in range(2):
                    dve.wait_ge(u_rounded[t], n + i + 1)
                    V.tensor_tensor(chunk(u_lo, 2 * i + t), y[:, t, :], as_f32(chunk(u_hi, 2 * i + t)), SUB).then_inc(u_split[t], 1)
                split_unit(1, m + i + 1, columns)

            def down_step(layer, j, columns):
                m = M_DOWN[layer]
                for t in range(2):
                    e = 2 * j + t
                    if columns[t]:
                        split_unit(0, m + e + 1, columns[t])
                    dve.wait_ge(unit_done[1], m + e + 1)
                    V.tensor_tensor(chunk(x_res, e), bank[t][:, :], chunk(x_res, e), ADD).then_inc(x_updated, 1)
                    split_x(e, "mix1" if layer == 0 else None, H_DOWN + e, Q_DOWN[layer] + e, S_DOWN[layer] + e, t)
                    if layer == 0:
                        dve.wait_ge(h_split, H_DOWN + e + 1)
                        V.tensor_scalar(chunk(x_res, e), chunk(x_res, e), pool_shift[:, bass.ds(e, 1)], None, ADD).then_inc(shifted, 1)
                    if columns[t]:
                        split_unit(1, m + e + 1, columns[t])

            for layer in range(DEPTH):
                if layer == 1:
                    dve.wait_ge(root_done, 3)
                    V.reciprocal(root_tok[:, :], root_tok[:, :]).then_inc(rms_ready, 1)
                    dve.wait_ge(rms_ready, 3)
                    clear_sums()
                    for group in range(len(WINDOWS)):
                        if group == 3:
                            split_unit(0, M_UP[1], UNIT)
                        for j in range(BLOCKS):
                            dve.wait_ge(map_rounded, BLOCKS * group + j // 2 * 2 + 2)
                            at_group = slice(group * GROUP, (group + 1) * GROUP)
                            V.scalar_tensor_tensor(map_lo[:, j, at_group], map_bank(group, j), root_tok[:, j:j + 1], as_f32(map_hi[:, j, at_group]), MUL, SUB).then_inc(map_split, 1)

                    def split_updated(c):
                        dve.wait_ge(h_rounded, H_POOL + c + 1)
                        V.scalar_tensor_tensor(h_lo[:, c, :], x_res[:, c, :], col("ffn1", c), as_f32(h_hi[:, c, :]), MUL, SUB).then_inc(h_split, 1)

                    dve.wait_ge(shifted, KD)
                    for c in range(KD):
                        w = WINDOWS[c // 2]
                        src, gain = bank[BANKS_WINDOW[c]], pool_gain[:, c:c + 1]
                        dve.wait_ge(window_mm, c + 1)
                        if c:
                            dve.wait_ge(start_added, c)
                        V.scalar_tensor_tensor(start_sum[:, 0:w - 1], src[:, 0:w - 1], float(w), inv_count[:, 0:w - 1], MUL, MUL).then_inc(start_scaled, 1)
                        dve.wait_ge(start_scaled, c + 1)
                        V.scalar_tensor_tensor(x_res[:, c, 0:w - 1], start_sum[:, 0:w - 1], gain, x_res[:, c, 0:w - 1], MUL, ADD).then_inc(start_added, 1)
                        dve.wait_ge(start_added, c + 1)
                        V.scalar_tensor_tensor(x_res[:, c, w - 1:T], src[:, w - 1:T], gain, x_res[:, c, w - 1:T], MUL, ADD).then_inc(x_updated, 1)
                        if c:
                            split_updated(c - 1)
                    split_updated(KD - 1)
                    V.memset(act_in[:, :, 0:2], 0.0).then_inc(memory_cleared, 1)
                    split_unit(1, M_UP[1], UNIT)
                    for c in range(KD):
                        dve.wait_ge(squared, Q_POOL + c + 1)
                        dve.wait_ge(summed, S_POOL + c + 1)
                        V.tensor_tensor(sumsq[:, :], sumsq[:, :], pool_sq[:, c, :], ADD).then_inc(summed, 1)
                    dve.wait_ge(memory_cleared, 1)
                inverse(1 if layer == 0 else 3)
                with dve.Fori(0, UP_STEPS - 1) as i:
                    up_step(layer, i, UNIT)
                up_step(layer, UP_STEPS - 1, DOWN_UNIT)
                clear_sums()
                with dve.Fori(0, DOWN_STEPS // 2 - 1) as j:
                    down_step(layer, j, (DOWN_UNIT, DOWN_UNIT))
                down_step(layer, DOWN_STEPS // 2 - 1, (DOWN_UNIT, POOL_UNIT if layer == 0 else 0))
            inverse(4)
            for c in range(KD):
                V.scalar_tensor_tensor(out_sb[:, c, :], x_res[:, c, :], col("final", c), rms[:, :], MUL, MUL).then_inc(out_ready, 1)

        @block.tensor
        def _(pe):
            M = nc.tensor

            def three_passes(dst, s, w_at, hi, lo, start, stop):
                a, b = w_hi[s][:, w_at:w_at + P], w_lo[s][:, w_at:w_at + P]
                M.matmul(dst, a, hi, start=start, stop=False)
                M.matmul(dst, a, lo, start=False, stop=False)
                return M.matmul(dst, b, hi, start=False, stop=stop)

            def unit(s, m, hi, lo, before=None):
                pe.wait_ge(w_split[s], m + 1)
                for k in range(KD):
                    if before:
                        before(k)
                    for t in range(2):
                        last = three_passes(bank[2 * s + t][:, :], s, (2 * k + t) * P, hi[:, k, :], lo[:, k, :], k == 0, k == KD - 1)
                last.then_inc(unit_done[s], 1)

            def wait_drained(banks, count):
                for b in banks:
                    pe.wait_ge(drained[b], count)

            def sum_channels(n):
                pe.wait_ge(summed, (KD + 1) * (n + 1))
                M.matmul(bank[BANK_SUM][:, :], ones[:, :], sumsq[:, :], start=True, stop=True).then_inc(stat_mm, 1)

            def h_chunks(first, at_once):
                def before(k):
                    if k == 0 or k >= at_once:
                        pe.wait_ge(h_split, first + max(k + 1, at_once))
                return before

            def v_chunks(first):
                def before(k):
                    pe.wait_ge(v_split, first + k + 1)
                return before

            def tensor_taps(i):
                n = PE_TAPS[i]
                for t in range(2):
                    pe.wait_ge(diag_ready[t], 2 * sum(PE_TAPS[:i + 1]))
                    pe.wait_ge(glu_split[t], i + 1)
                    if 1 <= i < PW1_STEPS - 1:
                        pe.wait_ge(conv_drained, 2 * (i - 1) + t + 1)
                    for k in range(n):
                        slot, dst = 2 * (i % 2) + t, bank[BANKS_CONV[i][t]][:, :]
                        hi, lo = glu_hi[:, slot, k:k + T], glu_lo[:, slot, k:k + T]
                        M.matmul(dst, diag_hi[i % 2][t][:, k, :], hi, start=k == 0, stop=False)
                        M.matmul(dst, diag_hi[i % 2][t][:, k, :], lo, start=False, stop=False)
                        last = M.matmul(dst, diag_lo[i % 2][t][:, k, :], hi, start=False, stop=k == n - 1)
                    last.then_inc(conv_mm[t], 1)

            def sum_for_mean(i):
                for c in (2 * i, 2 * i + 1):
                    pe.wait_ge(conv_drained, c + 1)
                    last = M.matmul(bank[BANK_MEAN][:, :], ones[:, :], conv_out[:, c, :], start=c == 0, stop=c == KD - 1)
                if i == PW1_STEPS - 1:
                    last.then_inc(mean_mm, 1)

            pe.wait_ge(consts_set, CONSTS)
            for i in range(PW1_STEPS):
                for s in range(2):
                    if i:
                        wait_drained((2 * s, 2 * s + 1), DRAINED_PW1 + i)
                    unit(s, M_PW1 + i, h_hi, h_lo, (lambda k: pe.wait_ge(h_split, H_IN + k + 1)) if i == 0 and s == 0 else None)
                    if i == 0 and s == 0:
                        sum_channels(0)
                if i >= 2:
                    sum_for_mean(i - 2)
                if i:
                    tensor_taps(i - 1)
            tensor_taps(PW1_STEPS - 1)
            sum_for_mean(PW1_STEPS - 2)
            sum_for_mean(PW1_STEPS - 1)

            for c in range(KD):
                pe.wait_ge(dev_squared, c + 1)
                M.matmul(bank[BANK_SUM][:, :], ones[:, :], sq[:, c % 2, :], start=c == 0, stop=c == KD - 1).then_inc(dev_summed, 1)

            for j in range(PW2_STEPS):
                for s in range(2):
                    if j:
                        pe.wait_ge(x_updated, X_PW2 + 4 * (j - 1) + 2 * s + 2)
                    unit(s, M_PW2 + j, v_hi, v_lo, v_chunks(0) if j == 0 and s == 0 else None)

            def up_step(layer, i, norm=None):
                h = h_chunks(H_PW2, 6) if layer == 0 else h_chunks(H_POOL, 2)
                for s in range(2):
                    wait_drained((2 * s, 2 * s + 1), DRAINED_UP[layer] + i)
                    unit(s, M_UP[layer] + i, h_hi, h_lo, h)
                    if s == 0 and norm is not None:
                        sum_channels(norm)

            def down_step(layer, j):
                for t in range(2):
                    e = 2 * j + t
                    pe.wait_ge(drained[t], DRAINED_UP[layer] + UP_STEPS)
                    pe.wait_ge(x_updated, X_DOWN[layer] + e - 1)
                    for s in range(2):
                        pe.wait_ge(w_split[s], M_DOWN[layer] + e + 1)
                        for b in range(2):
                            pe.wait_ge(u_split[b], UP_STEPS * layer + ((DOWN_K + 1) // 2 if s == 0 else UP_STEPS))
                        for k in range(DOWN_K):
                            kk = s * DOWN_K + k
                            last = three_passes(bank[t][:, :], s, k * P, u_hi[:, kk, :], u_lo[:, kk, :], kk == 0, kk == KF - 1)
                        last.then_inc(unit_done[s], 1)

            for layer in range(DEPTH):
                if layer == 1:
                    for group in range(len(WINDOWS)):
                        slot = group // 2
                        pe.wait_ge(w_split[slot], M_POOL + 1)
                        pe.wait_ge(h_split, H_DOWN + 2 * group + 2)
                        if group == 2:
                            pe.wait_ge(x_updated, X_DOWN[0] + KD - 1)
                        if group == 3:
                            pe.wait_ge(map_split, BLOCKS)
                        for j in range(BLOCKS):
                            for k in range(2):
                                c, at_w = 2 * group + k, ((group % 2) * 2 + k) * GROUP
                                tok_hi, tok_lo = h_hi[:, c, j * P:(j + 1) * P], h_lo[:, c, j * P:(j + 1) * P]
                                hi, lo = w_hi[slot][:, at_w:at_w + GROUP], w_lo[slot][:, at_w:at_w + GROUP]
                                first = M.matmul(map_bank(group, j), tok_hi, hi, start=k == 0, stop=False)
                                if group == 2 and j == 0 and k == 0:
                                    first.then_inc(unit_done[0], 1)
                                M.matmul(map_bank(group, j), tok_hi, lo, start=False, stop=False)
                                last = M.matmul(map_bank(group, j), tok_lo, hi, start=False, stop=k == 1)
                            last.then_inc(map_mm, 1)
                        if group == 0:
                            pe.wait_ge(summed, (KD + 1) * 3)
                            for j in range(BLOCKS):
                                last = M.matmul(bank[BANK_SUM][:, j:j + 1], sumsq[:, j * P:(j + 1) * P], ones[:, 0:1], start=True, stop=True)
                            last.then_inc(stat_mm, 1)
                    pe.wait_ge(band_rounded, 1)
                    for c in range(KD):
                        group, dst = c // 2, bank[BANKS_WINDOW[c]]
                        pe.wait_ge(map_split, BLOCKS * (group + 1))
                        if c == 1:
                            pe.wait_ge(x_updated, X_DOWN[0] + KD)
                        if c >= 5:
                            pe.wait_ge(x_updated, X_POOL + BANKS_WINDOW.index(BANKS_WINDOW[c]) + 1)
                        at_band = group * BAND
                        parts = [m[:, j, c * P:(c + 1) * P] for j in range(BLOCKS) for m in (map_hi, map_lo)]
                        for j, first_out, first_col in ((0, 0, P), (2, 2 * P, P), (1, P, P), (3, 2 * P, 0)):
                            for n in range(2):
                                product = M.matmul(dst[:, first_out:first_out + 2 * P], parts[2 * j + n], band[:, at_band + first_col:at_band + first_col + 2 * P],
                                                   start=j == 0 and n == 0, stop=False, skip_group_check=True)
                                if c == 0 and j == 0 and n == 0:
                                    product.then_inc(unit_done[1], 1)
                        at_start = len(WINDOWS) * BAND + group * START
                        for n in range(2):
                            last = M.matmul(dst[:, 0:START], parts[n], band[:, at_start:at_start + START], start=False, stop=n == 1, skip_group_check=True)
                        last.then_inc(window_mm, 1)
                up_step(layer, 0, norm=1 if layer == 0 else 3)
                with pe.Fori(1, UP_STEPS) as i:
                    up_step(layer, i)
                with pe.Fori(0, DOWN_STEPS // 2) as j:
                    down_step(layer, j)
            sum_channels(4)


def _columns(v):
    return v.reshape(-1, P).T


def _bands():
    import numpy as np
    token, position = np.arange(P)[:, None], np.arange(2 * P)[None, :]
    bands = [np.concatenate([np.zeros((P, P)), ((position >= token) & (position < token + w)) - w * (position == token)], axis=1) for w in WINDOWS]
    starts = [(position == token)[:, :START] * np.maximum(w - 1 - token, 0) for w in WINDOWS]
    return np.concatenate(bands + starts, axis=1).astype(np.float32)


def kernel(**inputs):
    import numpy as np
    import concourse.bacc as bacc
    from concourse.bass_utils import run_bass_kernel_spmd

    a = {k: np.asarray(v) for k, v in inputs.items()}
    w_dw = a["conv_w_dw"][0].reshape(TAPS, KD, P).transpose(2, 1, 0).reshape(P, KD * TAPS)
    ffn_dw = np.concatenate([a["ffn_w_dw"], a["ffn_b_dw"][:, None, :]], axis=1)
    ffn_dw = ffn_dw.reshape(DEPTH, 4, KF, P).transpose(3, 0, 2, 1).reshape(P, DEPTH * KF * 4)
    vecs = np.concatenate(
        [_columns(v) for v in (a["norm_mix"][0], a["norm_mix"][1], a["norm_ffn"][0], a["norm_ffn"][1], a["final_norm"],
                               a["conv_b_pw1"][0], a["conv_b_dw"][0], a["conv_ln_g"][0], a["conv_ln_b"][0],
                               a["conv_b_pw2"][0], a["pool_b"][0], a["pool_scale"][0])] + [w_dw, ffn_dw], axis=1)

    pw1 = a["conv_w_pw1"][0].reshape(KD, P, 2, PW1_STEPS, 2 * P).transpose(3, 2, 1, 0, 4).reshape(2 * PW1_STEPS, P, UNIT)
    pw2 = a["conv_w_pw2"][0].reshape(KD, P, 2 * PW2_STEPS, 2 * P).transpose(2, 1, 0, 3).reshape(2 * PW2_STEPS, P, UNIT)
    up = a["ffn_w_up"].reshape(DEPTH, KD, P, 2, UP_STEPS, 2 * P).transpose(0, 4, 3, 2, 1, 5).reshape(DEPTH * 2 * UP_STEPS, P, UNIT)
    down = a["ffn_w_down"].reshape(DEPTH, 2, DOWN_K, P, DOWN_STEPS, P).transpose(0, 4, 1, 3, 2, 5).reshape(DEPTH * 2 * DOWN_STEPS, P, DOWN_UNIT)
    pool = a["pool_w"][0].reshape(2, 2, 2, P, 2 * P).transpose(0, 3, 1, 2, 4).reshape(2, P, POOL_UNIT)

    arrays = {
        "x": a["x"][0].reshape(T, KD, P).transpose(2, 1, 0),
        "vecs": vecs,
        "ident": np.eye(P, dtype=np.float32),
        "band": _bands(),
        "w_pw1": pw1, "w_pw2": pw2, "w_up": up, "w_down": down, "w_pool": pool,
    }
    arrays = {k: np.ascontiguousarray(v) for k, v in arrays.items()}
    nc = bacc.Bacc("TRN2", target_bir_lowering=False, num_devices=1)
    args = [nc.dram_tensor(k, v.shape, mybir.dt.float32, kind="ExternalInput").ap() for k, v in arrays.items()]
    out = nc.dram_tensor("out", (P, KD, T), mybir.dt.float32, kind="ExternalOutput").ap()
    build(nc, *args, out)
    r = run_bass_kernel_spmd(nc, [arrays], core_ids=[0])
    return np.ascontiguousarray(r.results[0]["out"].transpose(2, 1, 0).reshape(1, T, D))
```

```python
import concourse.bass as bass
from concourse import mybir
from contextlib import ExitStack

P = 128
D = 1024
T = 512
FF = 2816
KD = D // P
KF = FF // P
UNIT = 8 * 2 * P
HALF = UNIT // 2
DOWN_K = KF // 2
DOWN_UNIT = DOWN_K * P
POOL_UNIT = 2 * 2 * 2 * P
TAPS = 31
PAD = TAPS - 1
WINDOWS = (2, 4, 8, 16)
GROUP = D // len(WINDOWS)
BLOCKS = T // P
BAND = 3 * P
START = 16
BAND_COLS = len(WINDOWS) * (BAND + START)
RMS_EPS = 1e-6
LN_EPS = 1e-5
DEPTH = 2

PW1_STEPS = 4
PW2_STEPS = 2
UP_STEPS = KF // 2
DOWN_STEPS = KD
M_PW1 = 0
M_PW2 = M_PW1 + PW1_STEPS
M_UP = [M_PW2 + PW2_STEPS, 0]
M_DOWN = [M_UP[0] + UP_STEPS, 0]
M_POOL = M_DOWN[0] + DOWN_STEPS
M_UP[1] = M_POOL + 1
M_DOWN[1] = M_UP[1] + UP_STEPS
DRAINED_PW1, DRAINED_UP = 0, (PW1_STEPS, PW1_STEPS + UP_STEPS)
X_PW2, X_DOWN, X_POOL = 0, (KD, 3 * KD), 2 * KD
H_IN, H_PW2, H_DOWN, H_POOL = 0, KD, 2 * KD, 3 * KD
Q_IN, Q_PW2, Q_DOWN, Q_POOL = 0, KD, (2 * KD, 4 * KD), 3 * KD
S_IN, S_PW2, S_DOWN, S_POOL = 0, KD + 1, (2 * (KD + 1), 4 * (KD + 1)), 3 * (KD + 1)

COL = {}
_at = 0
for _name, _n in [("mix0", KD), ("mix1", KD), ("ffn0", KD), ("ffn1", KD), ("final", KD), ("b_pw1", 2 * KD),
                  ("b_dw", KD), ("ln_g", KD), ("ln_b", KD), ("b_pw2", KD), ("pool_b", KD), ("pool_s", KD),
                  ("w_dw", KD * TAPS), ("ffn_dw", DEPTH * KF * 4)]:
    COL[_name] = _at
    _at += _n
N_COLS = _at

PE_TAPS = [12, 12, 12, 15]
DIAG_TAPS = [12, 12]
EXTRA_TAPS = PE_TAPS[3] - DIAG_TAPS[1]

SPLIT_TAPS = 26
EARLY_TAPS = 22

BANK_SUM, BANK_MEAN = 4, 7
BANKS_CONV = [(5, 6), (5, 6), (5, 6), (0, 1)]
BANKS_MAP = [(2, 3), (5, 6), (7, 0), (2, 3)]
BANKS_WINDOW = (4, 1, 5, 6, 7, 4, 5, 6)


def build(nc, x_in, vecs, ident_in, band_in, w_pw1, w_pw2, w_up, w_down, w_pool, out):
    f32, f32r = mybir.dt.float32, mybir.dt.float32r
    ALU, ACT = mybir.AluOpType, mybir.ActivationFunctionType
    MUL, ADD, SUB = ALU.mult, ALU.add, ALU.subtract

    ctx = ExitStack()
    with ctx:
        at = [nc.sbuf_base]

        def place(name, shape, dt, offset=None):
            size = 4
            for n in shape[1:]:
                size *= n
            size = (size + 31) // 32 * 32
            if offset is None:
                offset = at[0]
                at[0] += size
            return nc.alloc_sbuf_tensor_at(name, shape, dt, offset=offset)

        at[0] = (at[0] + 31) // 32 * 32
        par = place("par", [P, N_COLS], f32)
        ident = place("ident", [P, P], f32)
        ones = place("ones", [P, P], f32)
        eps = place("eps", [P, 2], f32)
        inv_count = place("inv_count", [P, 16], f32)
        root_tok = place("root_tok", [P, BLOCKS], f32)
        pool_gain = place("pool_gain", [P, KD], f32)
        pool_shift = place("pool_shift", [P, KD], f32)
        warm = place("warm", [P, 1], f32)
        start_sum = place("start_sum", [P, START], f32)
        x_res = place("x_res", [P, KD, T], f32)
        H_HI = at[0]
        h_hi = place("h_hi", [P, KD, T], f32r)
        H_LO = at[0]
        h_lo = place("h_lo", [P, KD, T], f32r)
        w_raw = [place(f"w_raw{s}", [P, UNIT], f32) for s in range(2)]
        w_hi = [place(f"w_hi{s}", [P, UNIT], f32r) for s in range(2)]
        w_lo = [place(f"w_lo{s}", [P, UNIT], f32r) for s in range(2)]
        rms = place("rms", [P, T], f32)
        sumsq = place("sumsq", [P, T], f32)
        sq = place("sq", [P, 2, T], f32)
        ACT_IN = at[0]
        factor_diag = sq[:, 0, :]
        act_in = place("act_in", [P, 2, 2 + T], f32)
        y = place("y", [P, 2, T], f32)
        U_HI = at[0]
        u_hi = place("u_hi", [P, KF, T], f32r)
        U_LO = at[0]
        u_lo = place("u_lo", [P, KF, T], f32r)
        v_hi, v_lo = u_lo[:, 0:KD, :], u_lo[:, KD:2 * KD, :]
        conv_out = place("conv_out", [P, KD, T], f32, U_HI)
        o = U_HI + KD * T * 4
        glu = place("glu", [P, 2, PAD + T], f32, o)
        glu_hi = place("glu_hi", [P, 4, PAD + T], f32r, o + 4352)
        glu_lo = place("glu_lo", [P, 4, PAD + T], f32r, o + 4352 + 8704)
        val, gate = y, act_in[:, :, 2:2 + T]
        o_taps = o + 5 * 4352
        tap_hi = place("tap_hi", [P, KD * TAPS], f32r, o_taps)
        tap_lo = place("tap_lo", [P, KD * TAPS], f32r, o_taps + 1024)
        o_diag = [o_taps + 2048, o_taps + 2048 + 4 * DIAG_TAPS[0] * P * 4]
        diag_hi = [[place(f"diag_hi{q}{t}", [P, DIAG_TAPS[q], P], f32r, o_diag[q] + t * DIAG_TAPS[q] * P * 4)
                    for t in range(2)] for q in range(2)]
        diag_lo = [[place(f"diag_lo{q}{t}", [P, DIAG_TAPS[q], P], f32r, o_diag[q] + (2 + t) * DIAG_TAPS[q] * P * 4)
                    for t in range(2)] for q in range(2)]
        assert o_diag[1] + 4 * DIAG_TAPS[1] * P * 4 <= U_HI + 2 * KF * T * 4
        extra_hi, extra_lo = [[place(f"extra_{part}{t}", [P, EXTRA_TAPS, P], f32r, H_LO + (2 * n + t) * EXTRA_TAPS * P * 4)
                               for t in range(2)] for n, part in enumerate(("hi", "lo"))]
        dev_sq = place("dev_sq", [P, KD, T], f32, H_HI)
        in_sq = place("in_sq", [P, KD, T], f32, U_HI)
        mean = place("mean", [P, T], f32, o)
        rstd = place("rstd", [P, T], f32, o + 2048)
        band_raw = place("band_raw", [P, BAND_COLS], f32, ACT_IN)
        band = place("band", [P, BAND_COLS], f32r, ACT_IN)
        map_hi = place("map_hi", [P, BLOCKS, D], f32r, U_HI)
        map_lo = place("map_lo", [P, BLOCKS, D], f32r, U_HI + BLOCKS * D * 4)
        pool_sq = place("pool_sq", [P, KD, T], f32, U_HI + 2 * BLOCKS * D * 4)
        out_sb = place("out_sb", [P, KD, T], f32, U_HI)

        bank = [ctx.enter_context(nc.psum_tensor(f"bank{b}", [P, T], f32)) for b in range(8)]

        def sem(name):
            return ctx.enter_context(nc.semaphore(name))

        def sems(name, n=2):
            return [sem(f"{name}{i}") for i in range(n)]

        par_loaded, ident_loaded, out_stored = sem("par_loaded"), sem("ident_loaded"), sem("out_stored")
        x_loaded = sems("x_loaded", 4)
        raw_loaded = sems("raw_loaded")
        w_rounded = sems("w_rounded")
        w_split = sems("w_split")
        unit_done = sems("unit_done")
        drained = sems("drained", 4)
        x_updated, h_rounded, h_split = sem("x_updated"), sem("h_rounded"), sem("h_split")
        squared, summed = sem("squared"), sem("summed")
        stat_mm, root_done, rms_ready = sem("stat_mm"), sem("root_done"), sem("rms_ready")
        tok_root, tok_factor, diag_set = sem("tok_root"), sem("tok_factor"), sem("diag_set")
        spread_mm, spread_read = sem("spread_mm"), sem("spread_read")
        half_loaded, half_rounded, half_split = sem("half_loaded"), sem("half_rounded"), sem("half_split")
        consts_set, memory_cleared = sem("consts_set"), sem("memory_cleared")
        taps_split, tap_rounded = sem("taps_split"), sem("tap_rounded")
        diag_ready = sems("diag_ready")
        gate_ready, glu_done = sems("gate_ready"), sems("glu_done")
        glu_rounded, glu_split = sems("glu_rounded"), sems("glu_split")
        tap_step = sems("tap_step")
        conv_mm, conv_drained = sems("conv_mm"), sem("conv_drained")
        mean_mm, mean_ready, centred = sem("mean_mm"), sem("mean_ready"), sem("centred")
        dev_squared, dev_paired, dev_summed = sem("dev_squared"), sem("dev_paired"), sem("dev_summed")
        normed, swished, v_rounded, v_split = sem("normed"), sem("swished"), sem("v_rounded"), sem("v_split")
        tap2_done, tap1_done, conv3_done = sems("tap2_done"), sems("tap1_done"), sems("conv3_done")
        silu_done, act_scaled = sems("silu_done"), sems("act_scaled")
        u_rounded, u_split = sems("u_rounded"), sems("u_split")
        band_loaded, band_rounded, pool_vecs = sem("band_loaded"), sem("band_rounded"), sem("pool_vecs")
        shifted = sem("shifted")
        map_mm, map_rounded, map_split = sem("map_mm"), sem("map_rounded"), sem("map_split")
        window_mm, start_scaled, start_added = sem("window_mm"), sem("start_scaled"), sem("start_added")
        out_ready = sem("out_ready")

        def col(name, i, n=1):
            return par[:, bass.ds(COL[name] + i, n)]

        def flat(ap):
            return ap.rearrange("p a t -> p (a t)")

        def chunk(tensor, c):
            return flat(tensor[:, bass.ds(c, 1), :])

        def as_f32(ap):
            return ap.bitcast(f32)

        def map_bank(group, j):
            return bank[BANKS_MAP[group][j // 2]][:, (j % 2) * GROUP:(j % 2 + 1) * GROUP]

        block = ctx.enter_context(nc.Block())

        @block.sync
        def _(sp):
            sp.dma_start(par[:, :], vecs).then_inc(par_loaded, 16)
            sp.dma_start(x_res[:, 0:2, :], x_in[:, 0:2, :]).then_inc(x_loaded[0], 16)

            def load_step(source, first, m, columns):
                for s in range(2):
                    sp.wait_ge(w_split[s], m)
                    sp.dma_start(w_raw[s][:, 0:columns], source[first + s]).then_inc(raw_loaded[s], 16)

            sp.dma_start(w_raw[0][:, 0:HALF], w_pw1[0][:, 0:HALF]).then_inc(half_loaded, 16)
            sp.dma_start(w_raw[0][:, HALF:UNIT], w_pw1[0][:, HALF:UNIT]).then_inc(raw_loaded[0], 16)
            for q in range(1, 4):
                sp.dma_start(x_res[:, 2 * q:2 * q + 2, :], x_in[:, 2 * q:2 * q + 2, :]).then_inc(x_loaded[q], 16)
            sp.dma_start(w_raw[1][:, :], w_pw1[1]).then_inc(raw_loaded[1], 16)
            sp.dma_start(ident[:, :], ident_in).then_inc(ident_loaded, 16)
            with sp.Fori(1, PW1_STEPS) as i:
                load_step(w_pw1, 2 * i, M_PW1 + i, UNIT)
            with sp.Fori(0, PW2_STEPS) as i:
                load_step(w_pw2, 2 * i, M_PW2 + i, UNIT)
            for layer in range(DEPTH):
                if layer == 1:
                    for t in range(2):
                        sp.wait_ge(u_split[t], UP_STEPS)
                    sp.dma_start(band_raw[:, :], band_in).then_inc(band_loaded, 16)
                    load_step(w_pool, 0, M_POOL, POOL_UNIT)
                with sp.Fori(0, UP_STEPS) as i:
                    load_step(w_up, 2 * i + 2 * UP_STEPS * layer, M_UP[layer] + i, UNIT)
                with sp.Fori(0, DOWN_STEPS) as e:
                    load_step(w_down, 2 * e + 2 * DOWN_STEPS * layer, M_DOWN[layer] + e, DOWN_UNIT)
            for c in range(KD):
                sp.wait_ge(out_ready, c + 1)
                sp.dma_start(out[:, c, :], out_sb[:, c, :]).then_inc(out_stored, 16)
            sp.wait_ge(out_stored, 16 * KD)

        @block.gpsimd
        def _(pool):
            nc.gpsimd.memset(ones[:, :], 1.0).then_inc(consts_set, 1)
            nc.gpsimd.memset(eps[:, 0:1], RMS_EPS).then_inc(consts_set, 1)
            nc.gpsimd.memset(eps[:, 1:2], LN_EPS).then_inc(consts_set, 1)
            nc.gpsimd.memset(act_in[:, :, 0:2], 0.0).then_inc(consts_set, 1)
            nc.gpsimd.memset(glu[:, :, 0:PAD], 0.0).then_inc(consts_set, 1)
            for t in range(max(WINDOWS) - 1):
                nc.gpsimd.memset(inv_count[:, t:t + 1], 1.0 / (t + 1)).then_inc(consts_set, 1)

        CONSTS = 5 + max(WINDOWS) - 1

        @block.scalar
        def _(act):
            def round_unit(s, m, columns):
                act.wait_ge(raw_loaded[s], 16 * (m + 1))
                act.wait_ge(unit_done[s], m)
                nc.scalar.activation(w_hi[s][:, 0:columns], w_raw[s][:, 0:columns], ACT.Copy).then_inc(w_rounded[s], 1)

            def round_x(c, norm, s_index, t):
                act.wait_ge(summed, s_index)
                nc.scalar.activation(sq[:, t, :], chunk(x_res, c), ACT.Square).then_inc(squared, 1)
                if norm is not None:
                    nc.scalar.activation(chunk(h_hi, c), chunk(x_res, c), ACT.Copy, scale=col(norm, c)).then_inc(h_rounded, 1)

            def root(n):
                act.wait_ge(stat_mm, n + 1)
                nc.scalar.activation(rms[:, :], bank[BANK_SUM][:, :], ACT.Sqrt, scale=1.0 / D, bias=eps[:, 0:1]).then_inc(root_done, 1)

            act.wait_ge(par_loaded, 16)
            act.wait_ge(consts_set, CONSTS)
            def square_in(c):
                nc.scalar.activation(in_sq[:, c, :], x_res[:, c, :], ACT.Square).then_inc(squared, 1)

            for c in range(KD):
                act.wait_ge(x_loaded[c // 2], 16)
                nc.scalar.activation(h_hi[:, c, :], x_res[:, c, :], ACT.Copy, scale=col("mix0", c)).then_inc(h_rounded, 1)
                if c == 1:
                    act.wait_ge(half_loaded, 16)
                    nc.scalar.activation(w_hi[0][:, 0:HALF], w_raw[0][:, 0:HALF], ACT.Copy).then_inc(half_rounded, 1)
                    act.wait_ge(raw_loaded[0], 16)
                    nc.scalar.activation(w_hi[0][:, HALF:UNIT], w_raw[0][:, HALF:UNIT], ACT.Copy).then_inc(w_rounded[0], 1)
                if c >= 2:
                    square_in(c - 2)
            act.wait_ge(raw_loaded[1], 16)
            nc.scalar.activation(w_hi[1][:, :], w_raw[1][:, :], ACT.Copy).then_inc(w_rounded[1], 1)
            square_in(KD - 2)
            square_in(KD - 1)
            nc.scalar.activation(tap_hi[:, :], par[:, COL["w_dw"]:COL["w_dw"] + KD * TAPS], ACT.Copy).then_inc(tap_rounded, 1)
            round_unit(0, M_PW1 + 1, UNIT)
            root(0)

            def touch_root():
                nc.scalar.activation(warm[:, :], eps[:, 0:1], ACT.Sqrt)

            def root_by_token(n, offset):
                nc.scalar.activation(root_tok[:, :], bank[BANK_SUM][:, 0:BLOCKS], ACT.Sqrt, scale=1.0 / D, bias=eps[:, offset:offset + 1]).then_inc(tok_root, 1)

            def read_spread(n, dst):
                act.wait_ge(spread_mm, n + 1)
                nc.scalar.activation(dst[:, :], bank[BANK_SUM][:, :], ACT.Copy).then_inc(spread_read, 1)

            def diagonals(i, t):
                if i == 0 and t == 0:
                    act.wait_ge(ident_loaded, 16)
                    act.wait_ge(taps_split, 1)
                if i >= 2:
                    act.wait_ge(conv_mm[t], i - 1)
                for k in range(DIAG_TAPS[i % 2]):
                    w = (2 * i + t) * TAPS + k
                    nc.scalar.activation(diag_hi[i % 2][t][:, k, :], ident[:, :], ACT.Copy, scale=as_f32(tap_hi[:, w:w + 1])).then_inc(diag_ready[t], 1)
                    nc.scalar.activation(diag_lo[i % 2][t][:, k, :], ident[:, :], ACT.Copy, scale=as_f32(tap_lo[:, w:w + 1])).then_inc(diag_ready[t], 1)

            for i in range(PW1_STEPS):
                for t in range(2):
                    act.wait_ge(drained[2 + t], DRAINED_PW1 + i + 1)
                    nc.scalar.activation(gate[:, t, :], gate[:, t, :], ACT.Sigmoid, bias=col("b_pw1", KD + 2 * i + t)).then_inc(gate_ready[t], 1)
                if i:
                    round_unit(0, M_PW1 + i + 1, UNIT)
                round_unit(1, M_PW1 + i + 1, UNIT)
                if i == PW1_STEPS - 1:
                    for t in range(2):
                        for k in range(EXTRA_TAPS):
                            w = (2 * i + t) * TAPS + DIAG_TAPS[i % 2] + k
                            nc.scalar.activation(extra_hi[t][:, k, :], ident[:, :], ACT.Copy, scale=as_f32(tap_hi[:, w:w + 1])).then_inc(diag_ready[t], 1)
                            nc.scalar.activation(extra_lo[t][:, k, :], ident[:, :], ACT.Copy, scale=as_f32(tap_lo[:, w:w + 1])).then_inc(diag_ready[t], 1)
                for t in range(2):
                    act.wait_ge(glu_done[t], i + 1)
                    if i >= 2:
                        act.wait_ge(conv_mm[t], i - 1)
                    nc.scalar.activation(glu_hi[:, 2 * (i % 2) + t, :], glu[:, t, :], ACT.Copy).then_inc(glu_rounded[t], 1)
                for pair in ((0,), (1, 2), (3,), ())[i]:
                    for t in range(2):
                        diagonals(pair, t)

            touch_root()
            act.wait_ge(mean_mm, 1)
            nc.scalar.activation(mean[:, :], bank[BANK_MEAN][:, :], ACT.Copy, scale=1.0 / D).then_inc(mean_ready, 1)
            for c in range(KD):
                act.wait_ge(centred, c + 1)
                nc.scalar.activation(dev_sq[:, c, :], conv_out[:, c, :], ACT.Square).then_inc(dev_squared, 1)
            act.wait_ge(dev_summed, 1)
            root_by_token(0, 1)
            nc.scalar.activation(warm[:, :], eps[:, 0:1], ACT.Silu)
            read_spread(0, rstd)
            for c in range(KD):
                act.wait_ge(normed, c + 1)
                nc.scalar.activation(conv_out[:, c, :], conv_out[:, c, :], ACT.Silu, scale=col("ln_g", c), bias=col("ln_b", c)).then_inc(swished, 1)
                act.wait_ge(swished, c + 1)
                nc.scalar.activation(v_hi[:, c, :], conv_out[:, c, :], ACT.Copy).then_inc(v_rounded, 1)

            def pw2_step(j, next_m):
                for s in range(2):
                    for t in range(2):
                        c = 4 * j + 2 * s + t
                        act.wait_ge(x_updated, X_PW2 + c + 1)
                        round_x(c, "ffn0", S_PW2 + c, t)
                    round_unit(s, next_m, UNIT)

            for j in range(PW2_STEPS):
                pw2_step(j, M_PW2 + j + 1)

            def up_step(layer, i, columns, first=False):
                m, f = M_UP[layer], DRAINED_UP[layer]
                n = layer * UP_STEPS
                if not first:
                    round_unit(0, m + i + 1, columns)
                for t in range(2):
                    act.wait_ge(drained[t], f + i + 1)
                    w = COL["ffn_dw"] + 4 * (layer * KF + t) + 8 * i
                    nc.scalar.activation(y[:, t, :], act_in[:, t, 2:2 + T], ACT.Identity,
                                         scale=par[:, bass.ds(w + 2, 1)], bias=par[:, bass.ds(w + 3, 1)]).then_inc(tap2_done[t], 1)
                for t in range(2):
                    act.wait_ge(conv3_done[t], n + i + 1)
                    nc.scalar.activation(y[:, t, :], y[:, t, :], ACT.Silu).then_inc(silu_done[t], 1)
                for t in range(2):
                    act.wait_ge(drained[2 + t], f + i + 1)
                    nc.scalar.activation(chunk(u_hi, 2 * i + t), y[:, t, :], ACT.Copy).then_inc(u_rounded[t], 1)
                round_unit(1, m + i + 1, columns)

            def down_step(layer, j, columns):
                m = M_DOWN[layer]
                for t in range(2):
                    round_unit(0, m + 2 * j + t + 1, columns[t])
                    act.wait_ge(x_updated, X_DOWN[layer] + 2 * j + t + 1)
                    round_x(2 * j + t, "mix1" if layer == 0 else None, S_DOWN[layer] + 2 * j + t, t)
                    round_unit(1, m + 2 * j + t + 1, columns[t])

            for layer in range(DEPTH):
                if layer == 1:
                    act.wait_ge(band_loaded, 16)
                    nc.scalar.activation(band[:, :], band_raw[:, :], ACT.Copy).then_inc(band_rounded, 1)
                    act.wait_ge(stat_mm, 3)
                    nc.scalar.activation(root_tok[:, :], bank[BANK_SUM][:, 0:BLOCKS], ACT.Sqrt, scale=1.0 / D, bias=eps[:, 0:1]).then_inc(root_done, 1)
                    act.wait_ge(rms_ready, 3)
                    for group in range(len(WINDOWS)):
                        if group == 3:
                            round_unit(0, M_UP[1], UNIT)
                        for j in range(BLOCKS):
                            act.wait_ge(map_mm, BLOCKS * group + j // 2 * 2 + 2)
                            nc.scalar.activation(map_hi[:, j, group * GROUP:(group + 1) * GROUP], map_bank(group, j), ACT.Copy, scale=root_tok[:, j:j + 1]).then_inc(map_rounded, 1)
                    for c in range(KD):
                        act.wait_ge(x_updated, X_POOL + c + 1)
                        nc.scalar.activation(h_hi[:, c, :], x_res[:, c, :], ACT.Copy, scale=col("ffn1", c)).then_inc(h_rounded, 1)
                        nc.scalar.activation(pool_sq[:, c, :], x_res[:, c, :], ACT.Square).then_inc(squared, 1)
                        if c == 5:
                            round_unit(1, M_UP[1], UNIT)
                round_unit(0, M_UP[layer] + 1, UNIT)
                if layer == 0:
                    root(1)
                else:
                    act.wait_ge(stat_mm, 4)
                    root_by_token(1, 0)
                    read_spread(1, rms)
                up_step(layer, 0, UNIT, first=True)
                with act.Fori(1, UP_STEPS - 1) as i:
                    up_step(layer, i, UNIT)
                up_step(layer, UP_STEPS - 1, DOWN_UNIT)
                with act.Fori(0, DOWN_STEPS // 2 - 1) as j:
                    down_step(layer, j, (DOWN_UNIT, DOWN_UNIT))
                j = DOWN_STEPS // 2 - 1
                touch_root()
                if layer == 0:
                    down_step(layer, j, (DOWN_UNIT, POOL_UNIT))
                else:
                    m = M_DOWN[1] + 2 * j + 1
                    for t in range(2):
                        if t == 0:
                            round_unit(0, m, DOWN_UNIT)
                        act.wait_ge(x_updated, X_DOWN[1] + 2 * j + t + 1)
                        round_x(2 * j + t, None, S_DOWN[1] + 2 * j + t, t)
                        if t == 0:
                            round_unit(1, m, DOWN_UNIT)
            act.wait_ge(stat_mm, 5)
            root_by_token(2, 0)
            read_spread(2, rms)

        @block.vector
        def _(dve):
            V = nc.vector

            def split_unit(s, m, columns):
                dve.wait_ge(w_rounded[s], m + 1)
                V.tensor_tensor(w_lo[s][:, 0:columns], w_raw[s][:, 0:columns], as_f32(w_hi[s][:, 0:columns]), SUB).then_inc(w_split[s], 1)

            def clear_sums():
                V.memset(sumsq[:, :], 0.0).then_inc(summed, 1)

            def split_x(c, norm, h_index, q_index, s_index, t):
                if norm is not None:
                    dve.wait_ge(h_rounded, h_index + 1)
                    V.scalar_tensor_tensor(chunk(h_lo, c), chunk(x_res, c), col(norm, c), as_f32(chunk(h_hi, c)), MUL, SUB).then_inc(h_split, 1)
                dve.wait_ge(squared, q_index + 1)
                dve.wait_ge(summed, s_index + 1)
                V.tensor_tensor(sumsq[:, :], sumsq[:, :], sq[:, t, :], ADD).then_inc(summed, 1)

            def inverse(n):
                dve.wait_ge(root_done, n + 1)
                V.reciprocal(rms[:, :], rms[:, :]).then_inc(rms_ready, 1)
                dve.wait_ge(rms_ready, n + 1)

            clear_sums()
            dve.wait_ge(par_loaded, 16)
            for c in range(KD):
                dve.wait_ge(x_loaded[c // 2], 16)
                dve.wait_ge(h_rounded, H_IN + c + 1)
                V.scalar_tensor_tensor(h_lo[:, c, :], x_res[:, c, :], col("mix0", c), as_f32(h_hi[:, c, :]), MUL, SUB).then_inc(h_split, 1)
                if c == 1:
                    dve.wait_ge(half_rounded, 1)
                    V.tensor_tensor(w_lo[0][:, 0:HALF], w_raw[0][:, 0:HALF], as_f32(w_hi[0][:, 0:HALF]), SUB).then_inc(half_split, 1)
                    dve.wait_ge(w_rounded[0], 1)
                    V.tensor_tensor(w_lo[0][:, HALF:UNIT], w_raw[0][:, HALF:UNIT], as_f32(w_hi[0][:, HALF:UNIT]), SUB).then_inc(w_split[0], 1)
            split_unit(1, M_PW1, UNIT)
            for c in range(KD):
                dve.wait_ge(squared, Q_IN + c + 1)
                dve.wait_ge(summed, S_IN + c + 1)
                V.tensor_tensor(sumsq[:, :], sumsq[:, :], in_sq[:, c, :], ADD).then_inc(summed, 1)
            dve.wait_ge(tap_rounded, 1)
            V.tensor_tensor(tap_lo[:, :], par[:, COL["w_dw"]:COL["w_dw"] + KD * TAPS], as_f32(tap_hi[:, :]), SUB).then_inc(taps_split, 1)
            split_unit(0, M_PW1 + 1, UNIT)
            inverse(0)

            def spread_factors(n):
                dve.wait_ge(tok_root, n + 1)
                V.reciprocal(root_tok[:, :], root_tok[:, :]).then_inc(tok_factor, 1)
                dve.wait_ge(tok_factor, n + 1)
                for j in range(BLOCKS):
                    V.tensor_scalar(factor_diag[:, j * P:(j + 1) * P], ident[:, :], root_tok[:, j:j + 1], None, MUL).then_inc(diag_set, 1)
                dve.wait_ge(spread_read, n + 1)

            dve.wait_ge(consts_set, CONSTS)
            dve.wait_ge(ident_loaded, 16)
            V.tensor_tensor(pool_shift[:, :], col("pool_b", 0, KD), col("pool_s", 0, KD), MUL).then_inc(pool_vecs, 1)
            for group, w in enumerate(WINDOWS):
                V.tensor_scalar(pool_gain[:, 2 * group:2 * group + 2], col("pool_s", 2 * group, 2), 1.0 / w, None, MUL).then_inc(pool_vecs, 1)

            steps_before = [sum(TAPS - n for n in PE_TAPS[:i]) for i in range(PW1_STEPS)]

            def taps(i, first=0, last=TAPS):
                for k in range(max(first, PE_TAPS[i]), last):
                    for t in range(2):
                        c = 2 * i + t
                        src, w = glu[:, t, k:k + T], col("w_dw", c * TAPS + k)
                        if k == PE_TAPS[i]:
                            V.tensor_scalar(conv_out[:, c, :], src, w, col("b_dw", c), MUL, ADD).then_inc(tap_step[t], 1)
                        else:
                            dve.wait_ge(tap_step[t], steps_before[i] + k - PE_TAPS[i])
                            V.scalar_tensor_tensor(conv_out[:, c, :], src, w, conv_out[:, c, :], MUL, ADD).then_inc(tap_step[t], 1)

            def conv_sum(i):
                for t in range(2):
                    dve.wait_ge(tap_step[t], steps_before[i] + TAPS - PE_TAPS[i])
                    dve.wait_ge(conv_mm[t], i + 1)
                    V.tensor_tensor(conv_out[:, 2 * i + t, :], bank[BANKS_CONV[i][t]][:, :], conv_out[:, 2 * i + t, :], ADD).then_inc(conv_drained, 1)

            def drain_pair(i):
                for b, dst in ((2, gate), (0, val)) if i else ((0, val), (2, gate)):
                    for t in range(2):
                        dve.wait_ge(unit_done[b // 2], M_PW1 + i + 1)
                        V.tensor_tensor(dst[:, t, :], bank[b + t][:, :], rms[:, :], MUL).then_inc(drained[b + t], 1)

            for i in range(PW1_STEPS):
                if i == 1:
                    taps(0, last=EARLY_TAPS)
                    drain_pair(1)
                    taps(0, first=EARLY_TAPS, last=SPLIT_TAPS)
                    for s in range(2):
                        split_unit(s, M_PW1 + 2, UNIT)
                    taps(0, first=SPLIT_TAPS)
                elif i:
                    taps(i - 1, last=EARLY_TAPS)
                    conv_sum(i - 2)
                    taps(i - 1, first=EARLY_TAPS)
                if i != 1:
                    drain_pair(i)
                for t in range(2):
                    dve.wait_ge(gate_ready[t], i + 1)
                    dve.wait_ge(drained[t], DRAINED_PW1 + i + 1)
                    if i:
                        dve.wait_ge(tap_step[t], steps_before[i - 1] + TAPS - PE_TAPS[i - 1])
                    V.scalar_tensor_tensor(glu[:, t, PAD:PAD + T], val[:, t, :], col("b_pw1", 2 * i + t), gate[:, t, :], ADD, MUL).then_inc(glu_done[t], 1)
                for s in ((1,), (), (0, 1), (0, 1))[i]:
                    split_unit(s, M_PW1 + i + 1, UNIT)
                for t in range(2):
                    dve.wait_ge(glu_rounded[t], i + 1)
                    slot = 2 * (i % 2) + t
                    V.tensor_tensor(glu_lo[:, slot, :], glu[:, t, :], as_f32(glu_hi[:, slot, :]), SUB).then_inc(glu_split[t], 1)
            taps(PW1_STEPS - 1, last=EARLY_TAPS)
            conv_sum(PW1_STEPS - 2)
            taps(PW1_STEPS - 1, first=EARLY_TAPS)
            conv_sum(PW1_STEPS - 1)

            dve.wait_ge(mean_ready, 1)
            for pair in range(PW1_STEPS + 1):
                if pair < PW1_STEPS:
                    for c in (2 * pair, 2 * pair + 1):
                        V.tensor_tensor(conv_out[:, c, :], conv_out[:, c, :], mean[:, :], SUB).then_inc(centred, 1)
                if pair:
                    dve.wait_ge(dev_squared, 2 * pair)
                    V.tensor_tensor(dev_sq[:, 2 * pair - 2, :], dev_sq[:, 2 * pair - 2, :], dev_sq[:, 2 * pair - 1, :], ADD).then_inc(dev_paired, 1)
            clear_sums()
            spread_factors(0)

            def split_v(c):
                dve.wait_ge(v_rounded, c + 1)
                V.tensor_tensor(v_lo[:, c, :], conv_out[:, c, :], as_f32(v_hi[:, c, :]), SUB).then_inc(v_split, 1)

            for c in range(KD):
                V.tensor_tensor(conv_out[:, c, :], conv_out[:, c, :], rstd[:, :], MUL).then_inc(normed, 1)
                if c >= 2:
                    split_v(c - 2)
            split_v(KD - 2)
            split_v(KD - 1)

            for j in range(PW2_STEPS):
                for s in range(2):
                    for t in range(2):
                        c = 4 * j + 2 * s + t
                        dve.wait_ge(unit_done[s], M_PW2 + j + 1)
                        V.scalar_tensor_tensor(x_res[:, c, :], bank[2 * s + t][:, :], col("b_pw2", c), x_res[:, c, :], ADD, ADD).then_inc(x_updated, 1)
                    for t in range(2):
                        c = 4 * j + 2 * s + t
                        split_x(c, "ffn0", H_PW2 + c, Q_PW2 + c, S_PW2 + c, t)
                    split_unit(s, M_PW2 + j + 1, UNIT)

            def up_step(layer, i, columns, first=False):
                m = M_UP[layer]
                n = layer * UP_STEPS
                w = [COL["ffn_dw"] + 4 * (layer * KF + t) + 8 * i for t in range(2)]
                for t in range(2):
                    dve.wait_ge(unit_done[0], m + i + 1)
                    V.tensor_tensor(act_in[:, t, 2:2 + T], bank[t][:, :], rms[:, :], MUL).then_inc(drained[t], 1)
                if not first:
                    split_unit(0, m + i + 1, columns)
                for t in range(2):
                    dve.wait_ge(tap2_done[t], n + i + 1)
                    V.scalar_tensor_tensor(y[:, t, :], act_in[:, t, 1:1 + T], par[:, bass.ds(w[t] + 1, 1)], y[:, t, :], MUL, ADD).then_inc(tap1_done[t], 1)
                for t in range(2):
                    dve.wait_ge(tap1_done[t], n + i + 1)
                    V.scalar_tensor_tensor(y[:, t, :], act_in[:, t, 0:T], par[:, bass.ds(w[t], 1)], y[:, t, :], MUL, ADD).then_inc(conv3_done[t], 1)
                for t in range(2):
                    dve.wait_ge(silu_done[t], n + i + 1)
                    V.tensor_tensor(y[:, t, :], y[:, t, :], rms[:, :], MUL).then_inc(act_scaled[t], 1)
                for t in range(2):
                    dve.wait_ge(act_scaled[t], n + i + 1)
                    dve.wait_ge(unit_done[1], m + i + 1)
                    V.tensor_tensor(y[:, t, :], bank[2 + t][:, :], y[:, t, :], MUL).then_inc(drained[2 + t], 1)
                for t in range(2):
                    dve.wait_ge(u_rounded[t], n + i + 1)
                    V.tensor_tensor(chunk(u_lo, 2 * i + t), y[:, t, :], as_f32(chunk(u_hi, 2 * i + t)), SUB).then_inc(u_split[t], 1)
                split_unit(1, m + i + 1, columns)

            def down_step(layer, j, columns):
                m = M_DOWN[layer]
                for t in range(2):
                    e = 2 * j + t
                    if columns[t]:
                        split_unit(0, m + e + 1, columns[t])
                    dve.wait_ge(unit_done[1], m + e + 1)
                    V.tensor_tensor(chunk(x_res, e), bank[t][:, :], chunk(x_res, e), ADD).then_inc(x_updated, 1)
                    split_x(e, "mix1" if layer == 0 else None, H_DOWN + e, Q_DOWN[layer] + e, S_DOWN[layer] + e, t)
                    if layer == 0:
                        dve.wait_ge(h_split, H_DOWN + e + 1)
                        V.tensor_scalar(chunk(x_res, e), chunk(x_res, e), pool_shift[:, bass.ds(e, 1)], None, ADD).then_inc(shifted, 1)
                    if columns[t]:
                        split_unit(1, m + e + 1, columns[t])

            for layer in range(DEPTH):
                if layer == 1:
                    dve.wait_ge(root_done, 3)
                    V.reciprocal(root_tok[:, :], root_tok[:, :]).then_inc(rms_ready, 1)
                    dve.wait_ge(rms_ready, 3)
                    clear_sums()
                    for group in range(len(WINDOWS)):
                        if group == 3:
                            split_unit(0, M_UP[1], UNIT)
                        for j in range(BLOCKS):
                            dve.wait_ge(map_rounded, BLOCKS * group + j // 2 * 2 + 2)
                            at_group = slice(group * GROUP, (group + 1) * GROUP)
                            V.scalar_tensor_tensor(map_lo[:, j, at_group], map_bank(group, j), root_tok[:, j:j + 1], as_f32(map_hi[:, j, at_group]), MUL, SUB).then_inc(map_split, 1)

                    def split_updated(c):
                        dve.wait_ge(h_rounded, H_POOL + c + 1)
                        V.scalar_tensor_tensor(h_lo[:, c, :], x_res[:, c, :], col("ffn1", c), as_f32(h_hi[:, c, :]), MUL, SUB).then_inc(h_split, 1)

                    dve.wait_ge(shifted, KD)
                    for c in range(KD):
                        w = WINDOWS[c // 2]
                        src, gain = bank[BANKS_WINDOW[c]], pool_gain[:, c:c + 1]
                        dve.wait_ge(window_mm, c + 1)
                        if c:
                            dve.wait_ge(start_added, c)
                        V.scalar_tensor_tensor(start_sum[:, 0:w - 1], src[:, 0:w - 1], float(w), inv_count[:, 0:w - 1], MUL, MUL).then_inc(start_scaled, 1)
                        dve.wait_ge(start_scaled, c + 1)
                        V.scalar_tensor_tensor(x_res[:, c, 0:w - 1], start_sum[:, 0:w - 1], gain, x_res[:, c, 0:w - 1], MUL, ADD).then_inc(start_added, 1)
                        dve.wait_ge(start_added, c + 1)
                        V.scalar_tensor_tensor(x_res[:, c, w - 1:T], src[:, w - 1:T], gain, x_res[:, c, w - 1:T], MUL, ADD).then_inc(x_updated, 1)
                        if c:
                            split_updated(c - 1)
                    split_updated(KD - 1)
                    V.memset(act_in[:, :, 0:2], 0.0).then_inc(memory_cleared, 1)
                    split_unit(1, M_UP[1], UNIT)
                    for c in range(KD):
                        dve.wait_ge(squared, Q_POOL + c + 1)
                        dve.wait_ge(summed, S_POOL + c + 1)
                        V.tensor_tensor(sumsq[:, :], sumsq[:, :], pool_sq[:, c, :], ADD).then_inc(summed, 1)
                    dve.wait_ge(memory_cleared, 1)
                split_unit(0, M_UP[layer] + 1, UNIT)
                if layer == 0:
                    inverse(1)
                else:
                    spread_factors(1)
                up_step(layer, 0, UNIT, first=True)
                with dve.Fori(1, UP_STEPS - 1) as i:
                    up_step(layer, i, UNIT)
                up_step(layer, UP_STEPS - 1, DOWN_UNIT)
                clear_sums()
                with dve.Fori(0, DOWN_STEPS // 2 - 1) as j:
                    down_step(layer, j, (DOWN_UNIT, DOWN_UNIT))
                down_step(layer, DOWN_STEPS // 2 - 1, (DOWN_UNIT, POOL_UNIT if layer == 0 else 0))
            spread_factors(2)
            for c in range(KD):
                V.scalar_tensor_tensor(out_sb[:, c, :], x_res[:, c, :], col("final", c), rms[:, :], MUL, MUL).then_inc(out_ready, 1)

        @block.tensor
        def _(pe):
            M = nc.tensor

            def three_passes(dst, s, w_at, hi, lo, start, stop):
                a, b = w_hi[s][:, w_at:w_at + P], w_lo[s][:, w_at:w_at + P]
                M.matmul(dst, a, hi, start=start, stop=False)
                M.matmul(dst, a, lo, start=False, stop=False)
                return M.matmul(dst, b, hi, start=False, stop=stop)

            def unit(s, m, hi, lo, before=None, whole=True):
                if whole:
                    pe.wait_ge(w_split[s], m + 1)
                for k in range(KD):
                    if before:
                        before(k)
                    for t in range(2):
                        last = three_passes(bank[2 * s + t][:, :], s, (2 * k + t) * P, hi[:, k, :], lo[:, k, :], k == 0, k == KD - 1)
                last.then_inc(unit_done[s], 1)

            def wait_drained(banks, count):
                for b in banks:
                    pe.wait_ge(drained[b], count)

            def sum_channels(n):
                pe.wait_ge(summed, (KD + 1) * (n + 1))
                M.matmul(bank[BANK_SUM][:, :], ones[:, :], sumsq[:, :], start=True, stop=True).then_inc(stat_mm, 1)

            def h_chunks(first, at_once):
                def before(k):
                    if k == 0 or k >= at_once:
                        pe.wait_ge(h_split, first + max(k + 1, at_once))
                return before

            def v_chunks(first):
                def before(k):
                    pe.wait_ge(v_split, first + k + 1)
                return before

            def tensor_taps(i):
                n = PE_TAPS[i]
                for t in range(2):
                    pe.wait_ge(diag_ready[t], 2 * (sum(PE_TAPS[:i]) + DIAG_TAPS[i % 2]))
                    pe.wait_ge(glu_split[t], i + 1)
                    if 1 <= i < PW1_STEPS - 1:
                        pe.wait_ge(conv_drained, 2 * (i - 1) + t + 1)
                    for k in range(n):
                        slot, dst = 2 * (i % 2) + t, bank[BANKS_CONV[i][t]][:, :]
                        hi, lo = glu_hi[:, slot, k:k + T], glu_lo[:, slot, k:k + T]
                        at_extra = k - DIAG_TAPS[i % 2]
                        if at_extra == 0:
                            pe.wait_ge(diag_ready[t], 2 * sum(PE_TAPS[:i + 1]))
                        if at_extra < 0:
                            tap, rest = diag_hi[i % 2][t][:, k, :], diag_lo[i % 2][t][:, k, :]
                        else:
                            tap, rest = extra_hi[t][:, at_extra, :], extra_lo[t][:, at_extra, :]
                        M.matmul(dst, tap, hi, start=k == 0, stop=False)
                        M.matmul(dst, tap, lo, start=False, stop=False)
                        last = M.matmul(dst, rest, hi, start=False, stop=k == n - 1)
                    last.then_inc(conv_mm[t], 1)

            def sum_by_token(src, start, stop):
                for j in range(BLOCKS):
                    last = M.matmul(bank[BANK_SUM][:, j:j + 1], src[:, j * P:(j + 1) * P], ones[:, 0:1], start=start and j == 0, stop=stop, skip_group_check=True)
                return last

            def spread(n):
                pe.wait_ge(diag_set, BLOCKS * (n + 1))
                M.matmul(bank[BANK_SUM][:, :], ones[:, :], factor_diag, start=True, stop=True).then_inc(spread_mm, 1)

            def first_chunks(k):
                pe.wait_ge(h_split, H_IN + k + 1)
                if k == 0:
                    pe.wait_ge(half_split, 1)
                if k == KD // 2:
                    pe.wait_ge(w_split[0], M_PW1 + 1)

            def first_norm(k):
                if k == 4:
                    sum_channels(0)

            def second_norm(k):
                if k == 5:
                    pe.wait_ge(summed, (KD + 1) * 4)
                    sum_by_token(sumsq[:, :], start=True, stop=True).then_inc(stat_mm, 1)
                if k == 7:
                    spread(1)

            def sum_for_mean(i):
                for c in (2 * i, 2 * i + 1):
                    pe.wait_ge(conv_drained, c + 1)
                    last = M.matmul(bank[BANK_MEAN][:, :], ones[:, :], conv_out[:, c, :], start=c == 0, stop=c == KD - 1)
                if i == PW1_STEPS - 1:
                    last.then_inc(mean_mm, 1)

            pe.wait_ge(consts_set, CONSTS)
            for i in range(PW1_STEPS):
                for s in range(2):
                    if i:
                        wait_drained((2 * s, 2 * s + 1), DRAINED_PW1 + i)
                    unit(s, M_PW1 + i, h_hi, h_lo, (first_chunks, first_norm)[s] if i == 0 else None, whole=i > 0 or s > 0)
                if i >= 2:
                    sum_for_mean(i - 2)
                if i:
                    tensor_taps(i - 1)
            tensor_taps(PW1_STEPS - 1)
            sum_for_mean(PW1_STEPS - 2)
            sum_for_mean(PW1_STEPS - 1)

            for pair in range(PW1_STEPS):
                pe.wait_ge(dev_paired, pair + 1)
                last = sum_by_token(dev_sq[:, 2 * pair, :], start=pair == 0, stop=pair == PW1_STEPS - 1)
            last.then_inc(dev_summed, 1)
            spread(0)

            for j in range(PW2_STEPS):
                for s in range(2):
                    if j:
                        pe.wait_ge(x_updated, X_PW2 + 4 * (j - 1) + 2 * s + 2)
                    unit(s, M_PW2 + j, v_hi, v_lo, v_chunks(0) if j == 0 and s == 0 else None)

            def up_step(layer, i, first=False):
                h = h_chunks(H_PW2, 6) if layer == 0 else h_chunks(H_POOL, 2)
                for s in range(2):
                    wait_drained((2 * s, 2 * s + 1), DRAINED_UP[layer] + i)
                    unit(s, M_UP[layer] + i, h_hi, h_lo, second_norm if first and layer == 1 and s == 1 else h)
                    if first and layer == 0 and s == 0:
                        sum_channels(1)

            def down_step(layer, j):
                for t in range(2):
                    e = 2 * j + t
                    pe.wait_ge(drained[t], DRAINED_UP[layer] + UP_STEPS)
                    pe.wait_ge(x_updated, X_DOWN[layer] + e - 1)
                    for s in range(2):
                        pe.wait_ge(w_split[s], M_DOWN[layer] + e + 1)
                        for b in range(2):
                            pe.wait_ge(u_split[b], UP_STEPS * layer + ((DOWN_K + 1) // 2 if s == 0 else UP_STEPS))
                        for k in range(DOWN_K):
                            kk = s * DOWN_K + k
                            last = three_passes(bank[t][:, :], s, k * P, u_hi[:, kk, :], u_lo[:, kk, :], kk == 0, kk == KF - 1)
                        last.then_inc(unit_done[s], 1)

            for layer in range(DEPTH):
                if layer == 1:
                    for group in range(len(WINDOWS)):
                        slot = group // 2
                        pe.wait_ge(w_split[slot], M_POOL + 1)
                        pe.wait_ge(h_split, H_DOWN + 2 * group + 2)
                        if group == 2:
                            pe.wait_ge(x_updated, X_DOWN[0] + KD - 1)
                        if group == 3:
                            pe.wait_ge(map_split, BLOCKS)
                        for j in range(BLOCKS):
                            for k in range(2):
                                c, at_w = 2 * group + k, ((group % 2) * 2 + k) * GROUP
                                tok_hi, tok_lo = h_hi[:, c, j * P:(j + 1) * P], h_lo[:, c, j * P:(j + 1) * P]
                                hi, lo = w_hi[slot][:, at_w:at_w + GROUP], w_lo[slot][:, at_w:at_w + GROUP]
                                first = M.matmul(map_bank(group, j), tok_hi, hi, start=k == 0, stop=False)
                                if group == 2 and j == 0 and k == 0:
                                    first.then_inc(unit_done[0], 1)
                                M.matmul(map_bank(group, j), tok_hi, lo, start=False, stop=False)
                                last = M.matmul(map_bank(group, j), tok_lo, hi, start=False, stop=k == 1)
                            last.then_inc(map_mm, 1)
                        if group == 0:
                            pe.wait_ge(summed, (KD + 1) * 3)
                            sum_by_token(sumsq[:, :], start=True, stop=True).then_inc(stat_mm, 1)
                    pe.wait_ge(band_rounded, 1)
                    for c in range(KD):
                        group, dst = c // 2, bank[BANKS_WINDOW[c]]
                        pe.wait_ge(map_split, BLOCKS * (group + 1))
                        if c == 1:
                            pe.wait_ge(x_updated, X_DOWN[0] + KD)
                        if c >= 5:
                            pe.wait_ge(x_updated, X_POOL + BANKS_WINDOW.index(BANKS_WINDOW[c]) + 1)
                        at_band = group * BAND
                        parts = [m[:, j, c * P:(c + 1) * P] for j in range(BLOCKS) for m in (map_hi, map_lo)]
                        for j, first_out, first_col in ((0, 0, P), (2, 2 * P, P), (1, P, P), (3, 2 * P, 0)):
                            for n in range(2):
                                product = M.matmul(dst[:, first_out:first_out + 2 * P], parts[2 * j + n], band[:, at_band + first_col:at_band + first_col + 2 * P],
                                                   start=j == 0 and n == 0, stop=False, skip_group_check=True)
                                if c == 0 and j == 0 and n == 0:
                                    product.then_inc(unit_done[1], 1)
                        at_start = len(WINDOWS) * BAND + group * START
                        for n in range(2):
                            last = M.matmul(dst[:, 0:START], parts[n], band[:, at_start:at_start + START], start=False, stop=n == 1, skip_group_check=True)
                        last.then_inc(window_mm, 1)
                up_step(layer, 0, first=True)
                with pe.Fori(1, UP_STEPS) as i:
                    up_step(layer, i)
                with pe.Fori(0, DOWN_STEPS // 2) as j:
                    down_step(layer, j)
            pe.wait_ge(summed, (KD + 1) * 5)
            sum_by_token(sumsq[:, :], start=True, stop=True).then_inc(stat_mm, 1)
            spread(2)


def _columns(v):
    return v.reshape(-1, P).T


def _bands():
    import numpy as np
    token, position = np.arange(P)[:, None], np.arange(2 * P)[None, :]
    bands = [np.concatenate([np.zeros((P, P)), ((position >= token) & (position < token + w)) - w * (position == token)], axis=1) for w in WINDOWS]
    starts = [(position == token)[:, :START] * np.maximum(w - 1 - token, 0) for w in WINDOWS]
    return np.concatenate(bands + starts, axis=1).astype(np.float32)


def kernel(**inputs):
    import numpy as np
    import concourse.bacc as bacc
    from concourse.bass_utils import run_bass_kernel_spmd

    a = {k: np.asarray(v) for k, v in inputs.items()}
    w_dw = a["conv_w_dw"][0].reshape(TAPS, KD, P).transpose(2, 1, 0).reshape(P, KD * TAPS)
    ffn_dw = np.concatenate([a["ffn_w_dw"], a["ffn_b_dw"][:, None, :]], axis=1)
    ffn_dw = ffn_dw.reshape(DEPTH, 4, KF, P).transpose(3, 0, 2, 1).reshape(P, DEPTH * KF * 4)
    vecs = np.concatenate(
        [_columns(v) for v in (a["norm_mix"][0], a["norm_mix"][1], a["norm_ffn"][0], a["norm_ffn"][1], a["final_norm"],
                               a["conv_b_pw1"][0], a["conv_b_dw"][0], a["conv_ln_g"][0], a["conv_ln_b"][0],
                               a["conv_b_pw2"][0], a["pool_b"][0], a["pool_scale"][0])] + [w_dw, ffn_dw], axis=1)

    pw1 = a["conv_w_pw1"][0].reshape(KD, P, 2, PW1_STEPS, 2 * P).transpose(3, 2, 1, 0, 4).reshape(2 * PW1_STEPS, P, UNIT)
    pw2 = a["conv_w_pw2"][0].reshape(KD, P, 2 * PW2_STEPS, 2 * P).transpose(2, 1, 0, 3).reshape(2 * PW2_STEPS, P, UNIT)
    up = a["ffn_w_up"].reshape(DEPTH, KD, P, 2, UP_STEPS, 2 * P).transpose(0, 4, 3, 2, 1, 5).reshape(DEPTH * 2 * UP_STEPS, P, UNIT)
    down = a["ffn_w_down"].reshape(DEPTH, 2, DOWN_K, P, DOWN_STEPS, P).transpose(0, 4, 1, 3, 2, 5).reshape(DEPTH * 2 * DOWN_STEPS, P, DOWN_UNIT)
    pool = a["pool_w"][0].reshape(2, 2, 2, P, 2 * P).transpose(0, 3, 1, 2, 4).reshape(2, P, POOL_UNIT)

    arrays = {
        "x": a["x"][0].reshape(T, KD, P).transpose(2, 1, 0),
        "vecs": vecs,
        "ident": np.eye(P, dtype=np.float32),
        "band": _bands(),
        "w_pw1": pw1, "w_pw2": pw2, "w_up": up, "w_down": down, "w_pool": pool,
    }
    arrays = {k: np.ascontiguousarray(v) for k, v in arrays.items()}
    nc = bacc.Bacc("TRN2", target_bir_lowering=False, num_devices=1)
    args = [nc.dram_tensor(k, v.shape, mybir.dt.float32, kind="ExternalInput").ap() for k, v in arrays.items()]
    out = nc.dram_tensor("out", (P, KD, T), mybir.dt.float32, kind="ExternalOutput").ap()
    build(nc, *args, out)
    r = run_bass_kernel_spmd(nc, [arrays], core_ids=[0])
    return np.ascontiguousarray(r.results[0]["out"].transpose(2, 1, 0).reshape(1, T, D))
```
